# Optimizing a Trainium2 kernel written in Bass

```python
import math
import jax, jax.numpy as jnp
from jax import lax
import numpy as np

D_MODEL = 1024
BATCH = 1
SEQ = 128
DEPTH = 2
DEC_BATCH = 1
DEC_SEQ = 512
PAST_LEN = 256

GRID_W = 64
Q_BLOCK = 128
ROPE_THETA = 10000.0
EPS = 1e-6
N_MOD = 6
HEAD_DIM = 64
MIX_W = D_MODEL
MLA_HEADS = 6
MLA_NOPE = 32
MLA_ROPE = 32
MLA_V = 64
KV_RANK = 128
GQA_HEADS = 6
GQA_KV_HEADS = 2
GQA_GROUP = GQA_HEADS // GQA_KV_HEADS
DIFF_HEADS = 4
DIFF_QK = 32
DIFF_V = 64
MLA_W = MLA_HEADS * MLA_V
GQA_W = GQA_HEADS * HEAD_DIM
DIFF_W = DIFF_HEADS * DIFF_V
IN_SIZES = (MLA_HEADS * (MLA_NOPE + MLA_ROPE), KV_RANK, MLA_ROPE,
            GQA_HEADS * HEAD_DIM, GQA_KV_HEADS * HEAD_DIM, GQA_KV_HEADS * HEAD_DIM,
            DIFF_HEADS * 2 * DIFF_QK, DIFF_HEADS * 2 * DIFF_QK, DIFF_HEADS * DIFF_V)
IN_COLS = sum(IN_SIZES)
N_GROUPS = 4
EXPERTS_PER_GROUP = 4
N_EXPERTS = N_GROUPS * EXPERTS_PER_GROUP
TOP_K = 2
D_FF_EXPERT = 256

kernel_name = 'hybrid_diffusion_prefix_trunk_step'

def rms_norm(x, g):
    xf = x.astype(jnp.float32)
    y = xf * lax.rsqrt(jnp.mean(xf * xf, axis=-1, keepdims=True) + EPS)
    return (y * g.astype(jnp.float32)).astype(x.dtype)

def axial_rope(n_tokens, rot_dim):
    rows = n_tokens // GRID_W
    row = jnp.repeat(jnp.arange(rows, dtype=jnp.float32), GRID_W)
    col = jnp.tile(jnp.arange(GRID_W, dtype=jnp.float32), rows)
    quarter = rot_dim // 4
    inv = ROPE_THETA ** (-jnp.arange(quarter, dtype=jnp.float32) / quarter)
    ang = jnp.concatenate([row[:, None] * inv, col[:, None] * inv], axis=-1)
    return jnp.cos(ang), jnp.sin(ang)

def apply_rope(x, cos, sin):
    half = x.shape[-1] // 2
    shape = (cos.shape[0],) + (1,) * (x.ndim - 3) + (half,)
    cos = cos.reshape(shape).astype(x.dtype)
    sin = sin.reshape(shape).astype(x.dtype)
    x1, x2 = x[..., :half], x[..., half:]
    return jnp.concatenate([x1 * cos - x2 * sin, x1 * sin + x2 * cos], axis=-1)

def attend(q, k, v):
    B, Sq, KH, G, dk = q.shape
    dv = v.shape[-1]
    nb = Sq // Q_BLOCK
    scale = dk ** -0.5
    qb = jnp.moveaxis(q.reshape(B, nb, Q_BLOCK, KH, G, dk), 1, 0)

    def one(qblk):
        s = jnp.einsum('bqhgd,bkhd->bhgqk', qblk, k).astype(jnp.float32) * scale
        p = jax.nn.softmax(s, axis=-1)
        return jnp.einsum('bhgqk,bkhe->bqhge', p.astype(v.dtype), v)

    o = lax.map(one, qb)
    return jnp.moveaxis(o, 0, 1).reshape(B, Sq, KH, G, dv)

def split_cols(z):
    out, start = [], 0
    for size in IN_SIZES:
        out.append(z[..., start:start + size])
        start += size
    return out

def token_tensors(h, w_in, kv_g, qn_g, kn_g, rope):
    B, S, _ = h.shape
    z = jnp.einsum('bsd,de->bse', h, w_in)
    pa, pckv, pkr, pqg, pkg, pvg, pqd, pkd, pvd = split_cols(z)
    q_a = pa.reshape(B, S, MLA_HEADS, MLA_NOPE + MLA_ROPE)
    ckv = rms_norm(pckv, kv_g)
    k_rope = pkr
    q_g = rms_norm(pqg.reshape(B, S, GQA_KV_HEADS, GQA_GROUP, HEAD_DIM), qn_g)
    k_g = rms_norm(pkg.reshape(B, S, GQA_KV_HEADS, HEAD_DIM), kn_g)
    v_g = pvg.reshape(B, S, GQA_KV_HEADS, HEAD_DIM)
    q_d = pqd.reshape(B, S, DIFF_HEADS, 2, DIFF_QK)
    k_d = pkd.reshape(B, S, DIFF_HEADS, 2, DIFF_QK)
    v_d = pvd.reshape(B, S, DIFF_HEADS, DIFF_V)
    if rope is not None:
        (c32, s32), (c64, s64) = rope
        q_a = jnp.concatenate([q_a[..., :MLA_NOPE], apply_rope(q_a[..., MLA_NOPE:], c32, s32)], axis=-1)
        k_rope = apply_rope(k_rope, c32, s32)
        q_g = apply_rope(q_g, c64, s64)
        k_g = apply_rope(k_g, c64, s64)
        q_d = apply_rope(q_d, c32, s32)
        k_d = apply_rope(k_d, c32, s32)
    return (q_a, q_g, q_d), (ckv, k_rope, k_g, v_g, k_d, v_d)

def mix(qs, kvs, w_uk, w_uv, lam_p, diff_g, lam_init, w_out):
    q_a, q_g, q_d = qs
    ckv, k_rope, k_g, v_g, k_d, v_d = kvs
    B, S = q_a.shape[:2]
    Sk = ckv.shape[1]
    k_nope = jnp.einsum('bkr,rhd->bkhd', ckv, w_uk)
    v_a = jnp.einsum('bkr,rhe->bkhe', ckv, w_uv)
    k_a = jnp.concatenate([k_nope, jnp.broadcast_to(k_rope[:, :, None, :], (B, Sk, MLA_HEADS, MLA_ROPE))], axis=-1)
    o_a = attend(q_a[:, :, :, None, :], k_a, v_a).reshape(B, S, MLA_W)
    o_g = attend(q_g, k_g, v_g).reshape(B, S, GQA_W)
    lp = lam_p.astype(jnp.float32)
    lam = jnp.exp(jnp.sum(lp[0] * lp[1])) - jnp.exp(jnp.sum(lp[2] * lp[3])) + lam_init
    o1 = attend(q_d[:, :, :, 0:1, :], k_d[:, :, :, 0], v_d)[:, :, :, 0]
    o2 = attend(q_d[:, :, :, 1:2, :], k_d[:, :, :, 1], v_d)[:, :, :, 0]
    o_d = rms_norm(o1.astype(jnp.float32) - lam * o2.astype(jnp.float32), diff_g) * (1.0 - lam_init)
    o_d = o_d.astype(o1.dtype).reshape(B, S, DIFF_W)
    o = jnp.concatenate([o_a, o_g, o_d], axis=-1)
    return jnp.einsum('bse,ed->bsd', o, w_out)

def hier_moe(h, w_grp, b_grp, w_rtr, b_rtr, w_gate, w_up, w_down):
    B, S, D = h.shape
    t = h.reshape(B * S, D)
    T = t.shape[0]
    g_prob = jax.nn.softmax((t @ w_grp + b_grp).astype(jnp.float32), axis=-1)
    g_top, g_idx = lax.top_k(g_prob, 1)
    e_logits = (t @ w_rtr + b_rtr).astype(jnp.float32).reshape(T, N_GROUPS, EXPERTS_PER_GROUP)
    e_sel = jnp.take_along_axis(e_logits, jnp.broadcast_to(g_idx[:, :, None], (T, 1, EXPERTS_PER_GROUP)), axis=1)[:, 0]
    e_top, e_idx = lax.top_k(jax.nn.softmax(e_sel, axis=-1), TOP_K)
    e_top = e_top / jnp.sum(e_top, axis=-1, keepdims=True)
    expert_id = g_idx * EXPERTS_PER_GROUP + e_idx
    weights = g_top * e_top
    gates = jnp.sum(jax.nn.one_hot(expert_id, N_EXPERTS, dtype=jnp.float32) * weights[..., None], axis=1)
    a = jnp.einsum('td,edf->tef', t, w_gate)
    u = jnp.einsum('td,edf->tef', t, w_up)
    hid = jax.nn.silu(a) * u * gates.astype(t.dtype)[..., None]
    y = jnp.einsum('tef,efd->td', hid, w_down)
    return y.reshape(B, S, D)

def block(x, cond, i, rope, ctx_kv, p):
    (norm1_g, norm2_g, w_mod, b_mod, w_in, kv_g, w_uk, w_uv, qn_g, kn_g, diff_lambda, diff_g, w_out,
     w_grp, b_grp, w_rtr, b_rtr, w_gate, w_up, w_down) = p
    mod = (jnp.einsum('bd,de->be', jax.nn.silu(cond), w_mod[i]) + b_mod[i]).reshape(cond.shape[0], N_MOD, D_MODEL)[:, :, None, :]
    shift1, scale1, gate1, shift2, scale2, gate2 = (mod[:, j] for j in range(N_MOD))
    h = rms_norm(x, norm1_g[i]) * (1 + scale1) + shift1
    qs, kv = token_tensors(h, w_in[i], kv_g[i], qn_g[i], kn_g[i], rope)
    if ctx_kv is None:
        kv_read = kv
    else:
        kv_read = tuple(jnp.concatenate([cached, own], axis=1) for cached, own in zip(ctx_kv, kv))
    lam_init = 0.8 - 0.6 * math.exp(-0.3 * i)
    x = x + gate1 * mix(qs, kv_read, w_uk[i], w_uv[i], diff_lambda[i], diff_g[i], lam_init, w_out[i])
    h = rms_norm(x, norm2_g[i]) * (1 + scale2) + shift2
    x = x + gate2 * hier_moe(h, w_grp[i], b_grp[i], w_rtr[i], b_rtr[i], w_gate[i], w_up[i], w_down[i])
    return x, kv

def setup_inputs(seed: int = 0) -> dict:
    key = jax.random.key(seed)
    ks = jax.random.split(key, 32)
    n = lambda k, shape, s=1.0: jax.random.normal(k, shape, jnp.float32) * s
    D = D_MODEL
    return {
        'x_prompt': n(ks[0], (BATCH, SEQ, D)),
        'x_sample': n(ks[1], (DEC_BATCH, DEC_SEQ, D)),
        'c': n(ks[2], (DEC_BATCH, D)),
        'cache_mla_ckv': n(ks[3], (DEC_BATCH, DEPTH, PAST_LEN, KV_RANK)),
        'cache_mla_krope': n(ks[4], (DEC_BATCH, DEPTH, PAST_LEN, MLA_ROPE)),
        'cache_gqa_k': n(ks[5], (DEC_BATCH, DEPTH, PAST_LEN, GQA_KV_HEADS, HEAD_DIM)),
        'cache_gqa_v': n(ks[6], (DEC_BATCH, DEPTH, PAST_LEN, GQA_KV_HEADS, HEAD_DIM)),
        'cache_diff_k': n(ks[7], (DEC_BATCH, DEPTH, PAST_LEN, DIFF_HEADS, 2, DIFF_QK)),
        'cache_diff_v': n(ks[8], (DEC_BATCH, DEPTH, PAST_LEN, DIFF_HEADS, DIFF_V)),
        'c_ctx': n(ks[9], (D,)),
        'norm1_g': 1.0 + n(ks[10], (DEPTH, D), 0.1),
        'norm2_g': 1.0 + n(ks[11], (DEPTH, D), 0.1),
        'w_mod': n(ks[12], (DEPTH, D, N_MOD * D), D ** -0.5),
        'b_mod': n(ks[13], (DEPTH, N_MOD * D), 0.02),
        'w_in': n(ks[14], (DEPTH, D, IN_COLS), D ** -0.5),
        'mla_kv_norm_g': 1.0 + n(ks[15], (DEPTH, KV_RANK), 0.1),
        'mla_w_uk': n(ks[16], (DEPTH, KV_RANK, MLA_HEADS, MLA_NOPE), KV_RANK ** -0.5),
        'mla_w_uv': n(ks[17], (DEPTH, KV_RANK, MLA_HEADS, MLA_V), KV_RANK ** -0.5),
        'gqa_q_norm_g': 1.0 + n(ks[18], (DEPTH, HEAD_DIM), 0.1),
        'gqa_k_norm_g': 1.0 + n(ks[19], (DEPTH, HEAD_DIM), 0.1),
        'diff_lambda': n(ks[20], (DEPTH, 4, DIFF_QK), 0.1),
        'diff_norm_g': 1.0 + n(ks[21], (DEPTH, DIFF_V), 0.1),
        'w_out': n(ks[22], (DEPTH, MIX_W, D), MIX_W ** -0.5),
        'moe_w_group': n(ks[23], (DEPTH, D, N_GROUPS), D ** -0.5),
        'moe_b_group': n(ks[24], (DEPTH, N_GROUPS), 0.01),
        'moe_w_router': n(ks[25], (DEPTH, D, N_EXPERTS), D ** -0.5),
        'moe_b_router': n(ks[26], (DEPTH, N_EXPERTS), 0.01),
        'moe_w_gate': n(ks[27], (DEPTH, N_EXPERTS, D, D_FF_EXPERT), D ** -0.5),
        'moe_w_up': n(ks[28], (DEPTH, N_EXPERTS, D, D_FF_EXPERT), D ** -0.5),
        'moe_w_down': n(ks[29], (DEPTH, N_EXPERTS, D_FF_EXPERT, D), D_FF_EXPERT ** -0.5),
        'final_norm_g': 1.0 + n(ks[30], (D,), 0.1),
    }

def reference(x_prompt, x_sample, c, cache_mla_ckv, cache_mla_krope, cache_gqa_k, cache_gqa_v,
              cache_diff_k, cache_diff_v, c_ctx, norm1_g, norm2_g, w_mod, b_mod, w_in,
              mla_kv_norm_g, mla_w_uk, mla_w_uv, gqa_q_norm_g, gqa_k_norm_g, diff_lambda, diff_norm_g,
              w_out, moe_w_group, moe_b_group, moe_w_router, moe_b_router, moe_w_gate, moe_w_up,
              moe_w_down, final_norm_g):
    p = (norm1_g, norm2_g, w_mod, b_mod, w_in, mla_kv_norm_g, mla_w_uk, mla_w_uv, gqa_q_norm_g,
         gqa_k_norm_g, diff_lambda, diff_norm_g, w_out, moe_w_group, moe_b_group, moe_w_router,
         moe_b_router, moe_w_gate, moe_w_up, moe_w_down)
    x = x_prompt
    ctx_states = []
    for i in range(DEPTH):
        x, kv = block(x, c_ctx[None, :], i, None, None, p)
        ctx_states.append(kv)
    y_prompt = rms_norm(x, final_norm_g)
    new_mla_ckv = jnp.stack([s[0] for s in ctx_states], axis=1)
    new_mla_krope = jnp.stack([s[1] for s in ctx_states], axis=1)
    new_gqa_k = jnp.stack([s[2] for s in ctx_states], axis=1)
    new_gqa_v = jnp.stack([s[3] for s in ctx_states], axis=1)
    new_diff_k = jnp.stack([s[4] for s in ctx_states], axis=1)
    new_diff_v = jnp.stack([s[5] for s in ctx_states], axis=1)
    n_lat = x_sample.shape[1]
    rope = (axial_rope(n_lat, MLA_ROPE), axial_rope(n_lat, HEAD_DIM))
    caches = (cache_mla_ckv, cache_mla_krope, cache_gqa_k, cache_gqa_v, cache_diff_k, cache_diff_v)
    x = x_sample
    for i in range(DEPTH):
        ctx_kv = tuple(cch[:, i] for cch in caches)
        x, _ = block(x, c, i, rope, ctx_kv, p)
    y_sample = rms_norm(x, final_norm_g)
    return (y_prompt, y_sample, new_mla_ckv, new_mla_krope, new_gqa_k, new_gqa_v, new_diff_k, new_diff_v)


_drawn_inputs = setup_inputs


def setup_inputs(seed=0):
    import zlib

    import numpy as np

    out = dict(_drawn_inputs(seed))
    spreads = {}
    factors = {'gqa_q_norm_g': 5.699, 'moe_b_group': 4.474, 'moe_b_router': 3.398}
    for name, (base, spread) in spreads.items():
        noise = np.random.default_rng([zlib.crc32(name.encode()), seed]).standard_normal(out[name].shape)
        drawn = base * np.exp(spread * noise) if base else spread * noise
        out[name] = __import__('jax').numpy.asarray(drawn.astype(out[name].dtype))
    for name, factor in factors.items():
        out[name] = (out[name] * factor).astype(out[name].dtype)
    return out
```

```python
from contextlib import ExitStack

import numpy as np
import concourse.bass as bass
from concourse import mybir

F32 = mybir.dt.float32
I32 = mybir.dt.int32
ALU = mybir.AluOpType
ACT = mybir.ActivationFunctionType
AX = mybir.AxisListType

P = 128
D = 1024
KC = D // P
DEPTH = 2
T_CTX, T_LAT, PAST = 128, 512, 256
NT = (T_CTX + T_LAT) // P
EPS = 1e-6
GRID_W = 64
ROPE_THETA = 10000.0
RANK = 128
HM, HG, GKV, GJ, HD = 6, 6, 2, 3, 4
FF = 256
NE, NGRP, EPG = 16, 4, 4
BLK = [(0, 512), (512, 928), (928, 1440), (1440, 1952)]
N_PAIR = 2 * NT * P
N_ET = (N_PAIR + NE * (P - 1)) // P
N_SLOT = N_ET * P
N_SMALL_IN = 20

NU = 2 + NT
KCOL = [0, 128, 768, 256, 384, 512, 640]
SEEN = [0, 1, 3, 4, 5, 6]
KEYS = NU * P

N_UNIT = HM + HG + 2 * HD


def score_map(h):
    if h < HM:
        return h // 2, h % 2, h // 2, h * 64, 64 ** -0.5
    if h < HM + HG:
        j, g = divmod(h - HM, GKV)
        return 3 + j, g, 3, 384 + g * 64, 64 ** -0.5
    m = h - HM - HG
    return 6 + m // 4, m % 4, 4 + m // 4, 512 + (m // 2) * 64, 32 ** -0.5


def out_column(h):
    if h < HM:
        return h * 64
    if h < HM + HG:
        j, g = divmod(h - HM, GKV)
        return 384 + (g * GJ + j) * 64
    return 768 + ((h - HM - HG) // 2) * 64


MAPS_OF_BLOCK = [[h for h in range(N_UNIT) if score_map(h)[0] == b] for b in range(8)]

WO_COLS = [(0, 384), (384, 768), (768, 1024)]
RING = 4
N_MOD = 12
MOD_MID = 6


def ring_uses():
    uses = [("mod", 0, j) for j in range(N_MOD)]
    for l in range(DEPTH):
        uses += [("in", l, b) for b in range(len(BLK))]
        uses += [("out", l, b) for b in range(len(WO_COLS))]
        if l + 1 < DEPTH:
            uses += [("mod", l + 1, j) for j in range(MOD_MID)]
        uses += [("moe", l, i) for i in range(N_ET)]
        if l + 1 < DEPTH:
            uses += [("mod", l + 1, j) for j in range(MOD_MID, N_MOD)]
    return uses


USES = ring_uses()
USE_AT = {u: g for g, u in enumerate(USES)}
USE_INC = [32 if u[0] == "moe" else 16 for u in USES]
USE_CUM = [sum(USE_INC[g % RING:g + 1:RING]) for g in range(len(USES))]


def trunk(nc, a, o):
    def scratch(name, shape, dt=F32):
        return nc.dram_tensor(name, shape, dt).ap()

    mod_rows = scratch("mod_rows", (DEPTH, 2, 6 * D))
    h_rows = scratch("h_rows", (NT * P, D))
    slot_token = scratch("slot_token", (N_SLOT, 1), I32)
    y_rows = scratch("y_rows", (N_SLOT, D))

    ctx = ExitStack()
    with ctx:
        def sb(name, cols, dt=F32):
            return ctx.enter_context(nc.sbuf_tensor(name, [P, cols], dt))

        def sem(name):
            return ctx.enter_context(nc.semaphore(name))

        x = sb("x", NT * D)
        hT_region = sb("hT_region", KC * NT * P)
        ring = sb("ring", RING * 4096)
        arena = sb("arena", 6 * KEYS + NU * 768 + NT * D)
        qz = sb("qz", 12 * P)
        work = sb("work", 3072)
        k_tok = sb("k_tok", 2 * 640)
        ckvT = sb("ckvT", P)
        ident = sb("ident", P)
        ones = sb("ones", P)
        tri = sb("tri", P)
        rope = sb("rope", NT * 96)
        kv_g = sb("kv_g", RANK)
        qn_g = sb("qn_g", 64)
        kn_g = sb("kn_g", 64)
        df_g = sb("df_g", 64)
        lam_in = sb("lam_in", 128)
        lconst = sb("lconst", 8)
        n1col = sb("n1col", KC)
        w_rt = sb("w_rt", KC * 20)
        b_rt = sb("b_rt", 20)
        wuk = sb("wuk", 3 * P)
        wuv = sb("wuv", 384)
        cond = sb("cond", KC * 2)
        cond_e = sb("cond_e", KC * 2)
        silu_c = sb("silu_c", KC * 2)
        modrow = sb("modrow", 2 * 512)
        modcol = sb("modcol", 2 * 2 * KC)
        small = sb("small", 160)
        negh = sb("negh", 16)
        desc = sb("desc", 4)
        k128 = sb("k128", NT)
        le = sb("le", NE * NE)
        lt = sb("lt", NT * NT)
        iota_t = sb("iota_t", N_ET)
        rout_w = sb("rout_w", 2 * NT)
        tok_id = sb("tok_id", NT, I32)
        slots_i = sb("slots_i", 2 * NT, I32)
        idx = sb("idx", N_ET, I32)
        experts_i = sb("experts_i", N_ET, I32)
        ps = ctx.enter_context(nc.psum_tensor("ps", [P, 8, 512], F32))

        x_t = [x[:, t * D:(t + 1) * D] for t in range(NT)]
        hT = hT_region[:].rearrange("p (c n) -> p c n", c=KC)
        slot = [ring[:, s * 4096:(s + 1) * 4096] for s in range(RING)]
        kT = arena[:, 0:6 * KEYS].rearrange("p (j n) -> p j n", j=6)
        V0 = 6 * KEYS
        V = arena[:, V0:V0 + NU * 768].rearrange("p (u n) -> p u n", u=NU)
        Q0 = V0 + NU * 768
        q_tok = [arena[:, Q0 + t * D:Q0 + (t + 1) * D] for t in range(NT)]
        gate1c, gate1l = modrow[:], arena[:, 0:1024]
        a2b = arena[:, 2048:4096].rearrange("p (k n) -> p k n", k=2)
        b2b = arena[:, 4096:6144].rearrange("p (k n) -> p k n", k=2)
        gate2b = arena[:, 6144:8192].rearrange("p (k n) -> p k n", k=2)
        gain_b = arena[:, 8192:9216]
        w_dn = [arena[:, 9216 + 2048 * s:9216 + 2048 * (s + 1)] for s in range(2)]
        y_out = [arena[:, 13312 + 1024 * s:13312 + 1024 * (s + 1)] for s in range(2)]
        hg = [hT_region[:, 1024 * s:1024 * (s + 1)] for s in range(2)]
        hgT = [hT_region[:, 2048 + 1024 * s:2048 + 1024 * (s + 1)].rearrange("p (c n) -> p c n", c=KC)
               for s in range(2)]
        y_in = [[hT_region[:, 2048 * s + 1024 * k:2048 * s + 1024 * (k + 1)] for k in range(2)]
                for s in range(2)]
        xn = [work[:, 1024 * s:1024 * (s + 1)] for s in range(2)]
        rope_c = work[:, 2048:2560]
        rope_s = work[:, 2560:3072]
        pr = [work[:, 768 * s:768 * (s + 1)] for s in range(2)]
        prT = [work[:, 1536 + 768 * s:1536 + 768 * (s + 1)] for s in range(2)]
        h2T = work[:, 0:1024].rearrange("p (c n) -> p c n", c=KC)
        h2 = work[:, 1024:2048]
        xo_tmp = work[:, 2048:2432]
        logits = work[:, 2944:3044].rearrange("p (t n) -> p t n", t=NT)
        sig = [work[:, 256 * s:256 * (s + 1)] for s in range(2)]
        hid = [work[:, 512 + 256 * s:512 + 256 * (s + 1)] for s in range(2)]
        hidT = [work[:, 1024 + 256 * s:1024 + 256 * (s + 1)].rearrange("p (c n) -> p c n", c=2)
                for s in range(2)]
        pair_q = [[qz[:, (2 * s + i) * P:(2 * s + i + 1) * P] for i in range(2)] for s in range(2)]
        quad_q = [[qz[:, (4 + 4 * s + i) * P:(5 + 4 * s + i) * P] for i in range(4)] for s in range(2)]
        ss1, rs1 = small[:, 0:5], small[:, 5:10]
        ss9, rs9 = small[:, 10:19], small[:, 20:29]
        inv9 = small[:, 30:39]
        mx = small[:, 40:42]
        negm = small[:, 42:44]
        sums = small[:, 44:84]
        rec = small[:, 84:86]
        lam4 = small[:, 86:90]
        lam = small[:, 90:91]
        ss4, rs4 = small[:, 92:96], small[:, 96:100]
        dsc = small[:, 100:101]
        ss2, rs2 = small[:, 104:109], small[:, 109:114]
        ssf, rsf = small[:, 114:119], small[:, 119:124]
        k_view = [k_tok[:, 640 * s:640 * (s + 1)] for s in range(2)]
        def mod_row(j):
            q, k = divmod(j % 8, 2)
            return modrow[32 * q:32 * q + 2, k * 512:(k + 1) * 512]
        mod_c = modcol[:].rearrange("p (j k c) -> p j k c", j=2, k=2)
        silu_v = silu_c[:].rearrange("p (k c) -> p k c", k=2)

        w_landed = [sem(f"w_landed{s}") for s in range(RING)]
        wd_landed = [sem(f"wd_landed{s}") for s in range(2)]
        s_setup_dma = sem("s_setup_dma")
        s_small = sem("s_small")
        s_cond = sem("s_cond")
        s_modbias = sem("s_modbias")
        s_rowout = [sem(f"s_rowout{s}") for s in range(3)]
        s_modcol = sem("s_modcol")
        s_ctxout = sem("s_ctxout")
        s_gate1 = sem("s_gate1")
        s_bcast = sem("s_bcast")
        s_hout = sem("s_hout")
        s_scatter = sem("s_scatter")
        s_idx = sem("s_idx")
        s_hg = [sem(f"s_hg{s}") for s in range(2)]
        s_yout = [sem(f"s_yout{s}") for s in range(2)]
        s_yin = [sem(f"s_yin{s}") for s in range(2)]
        s_final = sem("s_final")
        c_const = sem("c_const")
        c_cond = sem("c_cond")
        c_e = sem("c_e")
        x_ready = sem("x_ready")
        mod_done = sem("mod_done")
        mod_evac = sem("mod_evac")
        a1_ready = sem("a1_ready")
        ss1_ready = sem("ss1_ready")
        rs1_ready = sem("rs1_ready")
        xn_ready = sem("xn_ready")
        hT_done = sem("hT_done")
        hT_evac = sem("hT_evac")
        z_done = sem("z_done")
        z_used_d = sem("z_used_d")
        z_used_a = sem("z_used_a")
        ss9_ready = sem("ss9_ready")
        rs9_ready = sem("rs9_ready")
        k_ready = sem("k_ready")
        k1_done = sem("k1_done")
        k2_done = sem("k2_done")
        kA_evac = sem("kA_evac")
        kB_evac = sem("kB_evac")
        qt_done = sem("qt_done")
        qz_d = sem("qz_d")
        qz_a = sem("qz_a")
        s_done = sem("s_done")
        m_ready = sem("m_ready")
        exp_done = sem("exp_done")
        pt4_done = sem("pt4_done")
        pt5_done = sem("pt5_done")
        pt4_evac = sem("pt4_evac")
        pt5_evac = sem("pt5_evac")
        pv_done = sem("pv_done")
        o_evac = sem("o_evac")
        lam_s = sem("lam_s")
        lam_e = sem("lam_e")
        ss4_ready = sem("ss4_ready")
        rs4_ready = sem("rs4_ready")
        o_ready = sem("o_ready")
        oT_done = sem("oT_done")
        oT_evac_d = sem("oT_evac_d")
        oT_evac_a = sem("oT_evac_a")
        wo_done = sem("wo_done")
        xo_done = sem("xo_done")
        ss2_ready = sem("ss2_ready")
        rs2_ready = sem("rs2_ready")
        h2_ready = sem("h2_ready")
        h2T_done = sem("h2T_done")
        h2T_evac_d = sem("h2T_evac_d")
        h2T_evac_a = sem("h2T_evac_a")
        rt_done = sem("rt_done")
        lg_ready = sem("lg_ready")
        r_sub = sem("r_sub")
        r_exp = sem("r_exp")
        r_mask = sem("r_mask")
        r_count = sem("r_count")
        slots_ready = sem("slots_ready")
        experts_ready = sem("experts_ready")
        gt_done = sem("gt_done")
        gt_evac_d = sem("gt_evac_d")
        gt_evac_a = sem("gt_evac_a")
        gu_done = sem("gu_done")
        sig_done = sem("sig_done")
        hid_ready = sem("hid_ready")
        ht_done = sem("ht_done")
        ht_evac = sem("ht_evac")
        dn_done = sem("dn_done")
        y_evac_d = sem("y_evac_d")
        y_evac_a = sem("y_evac_a")
        f_ss = sem("f_ss")
        f_rs = sem("f_rs")
        f_out = sem("f_out")

        N_Q = NT * 8
        N_S = NT * N_UNIT
        N_S5 = (NT - 1) * N_UNIT

        block = ctx.enter_context(nc.Block())

        def row_b(v, n, parts=P):
            return v.unsqueeze(0).to_broadcast([parts, n])

        def key_norm_rows(pool, l, t, rsqrt):
            pool.wait_ge(ss9_ready, l * NT + t + 1)
            rsqrt(rs9, ss9, 9).then_inc(rs9_ready, 1)
            if t == 0:
                pool.wait_ge(k_ready, l * NT + 1)
                pool.wait_ge(z_used_a, l * 3 * NT + 3)
                kb = k_view[0]
                for dst, src in (
                        (o["new_mla_ckv"][0, l], kb[:, 0:128]),
                        (o["new_mla_krope"][0, l], kb[:, 160:192]),
                        (o["new_gqa_k"][0, l].rearrange("s g n -> s (g n)"), kb[:, 256:384]),
                        (o["new_diff_k"][0, l].rearrange("s h k n -> s (h k n)"), kb[:, 384:640]),
                        (o["new_gqa_v"][0, l].rearrange("s g n -> s (g n)"), V[:, 2, 384:512]),
                        (o["new_diff_v"][0, l].rearrange("s h n -> s (h n)"), V[:, 2, 512:768])):
                    pool.dma_start(dst, src).then_inc(s_ctxout, 16)

        def y_copy_a(act, l, i):
            act.wait_ge(dn_done, l * N_ET + i + 1)
            y_buffer_free(act, l, i)
            act.activation(y_out[i % 2][:, 512:1024], ps[:, 6, :], ACT.Copy).then_inc(y_evac_a, 1)

        def y_buffer_free(eng, l, i):
            if i >= 2:
                n = ((N_ET + 1) // 2, N_ET // 2)[i % 2]
                eng.wait_ge(s_yout[i % 2], l * (16 * n) + 16 * (i // 2))

        RT = [0]

        def rt(n, base=work):
            v = base[:, RT[0]:RT[0] + n]
            RT[0] += n
            return v

        def v3(v, n):
            return v.rearrange("p (t n) -> p t n", n=n)

        def v4(v):
            return v.rearrange("p (t g e) -> p t g e", t=NT, g=NGRP)
        r_gm, r_gs, r_gex, r_gtop = rt(5), rt(20), rt(20), rt(5)
        r_t1, r_t2, r_t3, r_og = rt(20), rt(20), rt(5), rt(20)
        r_sel, r_es, r_m1, r_m2, r_o1, r_o2 = rt(80), rt(20), rt(5), rt(5), rt(20), rt(20)
        r_es2, r_d, r_ex2, r_den = rt(20), rt(5), rt(5), rt(5)
        r_O1, r_O2, r_M = rt(80), rt(80), rt(80)
        r_cn, r_rank, r_big, r_add = rt(80), rt(80), rt(400), rt(80)
        r_c, r_nt, r_incl, r_excl = rt(16), rt(16), rt(16), rt(16)
        r_sl, r_ex = rt(10), rt(N_ET)
        assert RT[0] <= 2048

        @block.sync
        def _(sp):
            for g, (kind, l, i) in enumerate(USES):
                if kind == "moe" and i == 0:
                    sp.wait_ge(experts_ready, l + 1)
                if kind == "moe":
                    e = sp.snap(l * NE + sp.value_load(experts_i[0:1, i:i + 1], min_val=0, max_val=NE - 1))
                if g >= RING:
                    uk, ul, ui = USES[g - RING]
                    if uk == "mod":
                        sp.wait_ge(mod_done, ul * N_MOD + ui + 1)
                    elif uk == "in":
                        sp.wait_ge(z_done, ul * 4 * NT + 4 * (NT - 1) + ui + 1)
                    elif uk == "out":
                        sp.wait_ge(wo_done, ul * 15 + 3 * (NT - 1) + ui + 1)
                    else:
                        sp.wait_ge(gu_done, ul * N_ET + ui + 1)
                to = slot[g % RING]
                if kind == "moe":
                    dst = to.rearrange("p (c k n) -> p c k n", c=KC, k=2)
                    for k, name in enumerate(("moe_w_gate", "moe_w_up")):
                        sp.dma_start(dst[:, :, k, :],
                                     a[name].rearrange("l e (p c) f -> (l e) p c f", c=KC)[e]
                                     ).then_inc(w_landed[g % RING], 16)
                    if i >= 2:
                        sp.wait_ge(dn_done, l * N_ET + i - 1)
                    else:
                        sp.wait_ge(wo_done, l * 15 + 15)
                    sp.dma_start(w_dn[i % 2].rearrange("p (c n) -> p c n", c=2),
                                 a["moe_w_down"].rearrange("l e (p c) n -> (l e) p c n", c=2)[e]
                                 ).then_inc(wd_landed[i % 2], 16)
                    continue
                name, (c0, c1) = {"mod": ("w_mod", (i * 512, (i + 1) * 512)), "in": ("w_in", BLK[min(i, 3)]),
                                  "out": ("w_out", WO_COLS[min(i, 2)])}[kind]
                sp.dma_start(to[:, 0:KC * (c1 - c0)].rearrange("p (c n) -> p c n", c=KC),
                             a[name][l].rearrange("(p c) n -> p c n", c=KC)[:, :, c0:c1]
                             ).then_inc(w_landed[g % RING], 16)

        @block.gpsimd
        def _(pool):
            dma = pool.dma_start
            dma(x_t[0], a["x_prompt"][0]).then_inc(s_setup_dma, 16)
            dma(x[:, D:].rearrange("p (t n) -> p t n", t=NT - 1),
                a["x_sample"][0].rearrange("(t p) n -> p t n", p=P)).then_inc(s_setup_dma, 16)
            for l in range(DEPTH):
                for k in range(2):
                    dma(mod_rows[l, k], a["b_mod"][l]).then_inc(s_modbias, 16)
            dma(rope[:].rearrange("p (t n) -> p t n", t=NT),
                a["rope_table"].rearrange("(t p) n -> p t n", p=P)).then_inc(s_setup_dma, 16)
            for v in (ident[:], wuk[:], qz[:], k_tok[:], idx[:]):
                pool.memset(v, 0.0 if v is not None and v.dtype == F32 else 0)
            pool.memset(tri[:], 1.0)
            pool.memset(ones[:], 1.0)
            pool.memset(le[:], 1.0)
            pool.memset(lt[:], 1.0)
            pool.memset(negh[:], -0.5)
            pool.memset(inv9[:, 0:1], 1.0 / RANK)
            pool.memset(inv9[:, 1:9], 1.0 / 64)
            pool.iota(desc[:], pattern=[[-1, 4]], base=4, channel_multiplier=0,
                      allow_small_or_imprecise_dtypes=True)
            pool.iota(k128[:], pattern=[[P, NT]], base=0, channel_multiplier=0,
                      allow_small_or_imprecise_dtypes=True)
            pool.iota(iota_t[:], pattern=[[1, N_ET]], base=0, channel_multiplier=0,
                      allow_small_or_imprecise_dtypes=True)
            pool.iota(tok_id[:], pattern=[[P, NT]], base=0, channel_multiplier=1)
            pool.drain()
            pool.affine_select(out=ident[:], in_=ident[:], compare_op=ALU.not_equal, fill=1.0, base=0,
                               pattern=[[-1, P]], channel_multiplier=1)
            pool.affine_select(out=tri[:], in_=tri[:], compare_op=ALU.is_gt, fill=0.0, base=0,
                               pattern=[[1, P]], channel_multiplier=-1)
            pool.affine_select(out=lt[:], in_=lt[:], compare_op=ALU.is_gt, fill=0.0, base=0,
                               pattern=[[1, NT], [-1, NT]], channel_multiplier=0)
            pool.affine_select(out=le[:], in_=le[:], compare_op=ALU.is_ge, fill=0.0, base=0,
                               pattern=[[1, NE], [-1, NE]], channel_multiplier=0)
            dma(slot_token.rearrange("(p i) one -> p (i one)", p=P), idx[:]).then_inc(s_setup_dma, 16)
            pool.drain()
            pool.sem_inc(c_const, 1)

            def rsqrt(out, v, n):
                pool.tensor_scalar(v, v, EPS, None, ALU.add)
                pool.drain()
                return pool.tensor_tensor(out, v, negh[:, 0:n], ALU.pow)

            def mod_store(l, j):
                pool.wait_ge(mod_evac, l * N_MOD + j + 1)
                dma(mod_rows[l, :, j * 512:(j + 1) * 512], mod_row(j), accum_op=ALU.add
                    ).then_inc(s_rowout[j // 4], 16)

            def mod_columns(l):
                pool.wait_ge(s_rowout[0], 64 * (l + 1))
                if l >= 1:
                    pool.wait_ge(hT_evac, l * 2 * NT + 1)
                for k in range(2):
                    dma(mod_c[:, :, k, :],
                        mod_rows[l, k, 0:2 * D].rearrange("(j p c) -> p j c", j=2, c=KC)
                        ).then_inc(s_modcol, 16)

            pool.wait_ge(s_modbias, 64)
            for l in range(DEPTH):
                pool.wait_ge(x_ready, l * NT + NT)
                small_in = [
                    (kv_g[:], row_b(a["mla_kv_norm_g"][l], RANK)),
                    (qn_g[:], row_b(a["gqa_q_norm_g"][l], 64)),
                    (kn_g[:], row_b(a["gqa_k_norm_g"][l], 64)),
                    (df_g[:], row_b(a["diff_norm_g"][l], 64)),
                    (lam_in[:], row_b(a["diff_lambda"].rearrange("l a b -> l (a b)")[l], 128)),
                    (lconst[:], row_b(a["layer_consts"][l], 8)),
                    (n1col[:], a["norm1_g"].rearrange("l (p c) -> l p c", c=KC)[l]),
                    (w_rt[:].rearrange("p (c n) -> p c n", c=KC)[:, :, 0:4],
                     a["moe_w_group"].rearrange("l (p c) n -> l p c n", c=KC)[l]),
                    (w_rt[:].rearrange("p (c n) -> p c n", c=KC)[:, :, 4:20],
                     a["moe_w_router"].rearrange("l (p c) n -> l p c n", c=KC)[l]),
                    (b_rt[:, 0:4], row_b(a["moe_b_group"][l], 4)),
                    (b_rt[:, 4:20], row_b(a["moe_b_router"][l], 16)),
                    (wuk[:].rearrange("p (h n) -> p h n", h=HM)[:, :, 0:32], a["mla_w_uk"][l]),
                    (wuv[:], a["mla_w_uv"].rearrange("l r h e -> l r (h e)")[l]),
                    (k_tok[:].rearrange("p (b n) -> p b n", b=2)[:, :, 0:128],
                     a["cache_mla_ckv"][0, l].rearrange("(b p) n -> p b n", p=P)),
                    (k_tok[:].rearrange("p (b n) -> p b n", b=2)[:, :, 160:192],
                     a["cache_mla_krope"][0, l].rearrange("(b p) n -> p b n", p=P)),
                    (k_tok[:].rearrange("p (b n) -> p b n", b=2)[:, :, 224:256],
                     a["cache_mla_krope"][0, l].rearrange("(b p) n -> p b n", p=P)),
                    (k_tok[:].rearrange("p (b n) -> p b n", b=2)[:, :, 256:384],
                     a["cache_gqa_k"][0, l].rearrange("(b p) g n -> p b (g n)", p=P)),
                    (k_tok[:].rearrange("p (b n) -> p b n", b=2)[:, :, 384:640],
                     a["cache_diff_k"][0, l].rearrange("(b p) h k n -> p b (h k n)", p=P)),
                    (V[:, 0:2, 384:512], a["cache_gqa_v"][0, l].rearrange("(b p) g n -> p b (g n)", p=P)),
                    (V[:, 0:2, 512:768], a["cache_diff_v"][0, l].rearrange("(b p) h n -> p b (h n)", p=P)),
                ]
                assert len(small_in) == N_SMALL_IN
                for dst, src in small_in:
                    dma(dst, src).then_inc(s_small, 16)

                if l == 0:
                    for j in range(N_MOD):
                        mod_store(0, j)
                        if j == 3:
                            mod_columns(0)

                for t in range(NT):
                    pool.wait_ge(ss1_ready, l * NT + t + 1)
                    rsqrt(rs1[:, t:t + 1], ss1[:, t:t + 1], 1).then_inc(rs1_ready, 1)
                    if t >= 1:
                        key_norm_rows(pool, l, t - 1, rsqrt)
                key_norm_rows(pool, l, NT - 1, rsqrt)

                for t in range(NT):
                    pool.wait_ge(ss4_ready, l * NT + t + 1)
                    rsqrt(rs4, ss4, 4).then_inc(rs4_ready, 1)

                for k in range(3):
                    pool.wait_ge(s_rowout[k], 64 * (l + 1))
                dma(gate1c, row_b(mod_rows[l, 0, 2 * D:3 * D], D)).then_inc(s_gate1, 16)
                pool.wait_ge(pv_done, l * N_S + N_S)
                pool.wait_ge(s_ctxout, l * 96 + 96)
                dma(gate1l, row_b(mod_rows[l, 1, 2 * D:3 * D], D)).then_inc(s_gate1, 16)

                def rows(dst, j):
                    for k in range(2):
                        dma(dst[:, k, :], row_b(mod_rows[l, k, j * D:(j + 1) * D], D)
                            ).then_inc(s_bcast, 16)
                rows(a2b, 4)
                rows(b2b, 3)
                rows(gate2b, 5)
                dma(gain_b, row_b(a["norm2_g"][l], D)).then_inc(s_bcast, 16)

                for t in range(NT):
                    pool.wait_ge(ss2_ready, l * NT + t + 1)
                    rsqrt(rs2[:, t:t + 1], ss2[:, t:t + 1], 1).then_inc(rs2_ready, 1)
                    pool.wait_ge(h2_ready, l * NT + t + 1)
                    dma(h_rows[t * P:(t + 1) * P, :], h2).then_inc(s_hout, 16)

                if l + 1 < DEPTH:
                    mod_store(l + 1, 0)
                pool.wait_ge(slots_ready, l + 1)
                for k in range(2):
                    for t in range(NT):
                        c = k * NT + t
                        pool.indirect_dma_start(
                            out=slot_token, out_offset=bass.IndirectOffsetOnAxis(ap=slots_i[:, c:c + 1], axis=0),
                            in_=tok_id[:, t:t + 1], in_offset=None).then_inc(s_scatter, 16)
                pool.wait_ge(s_scatter, l * 160 + 160)
                dma(idx[:], slot_token.rearrange("(i p) one -> p (i one)", p=P), allow_slow_non_contiguous=True).then_inc(s_idx, 16)
                pool.wait_ge(s_idx, l * 16 + 16)
                pool.wait_ge(s_hout, l * 80 + 80)

                def y_store(i):
                    pool.wait_ge(y_evac_d, l * N_ET + i + 1)
                    pool.wait_ge(y_evac_a, l * N_ET + i + 1)
                    dma(y_rows[i * P:(i + 1) * P, :], y_out[i % 2]).then_inc(s_yout[i % 2], 16)

                for i in range(N_ET):
                    if i < 2:
                        pool.wait_ge(wo_done, l * 15 + 15)
                    else:
                        pool.wait_ge(gt_done, l * N_ET + i - 1)
                    pool.indirect_dma_start(
                        out=hg[i % 2], out_offset=None, in_=h_rows,
                        in_offset=bass.IndirectOffsetOnAxis(ap=idx[:, i:i + 1], axis=0)).then_inc(s_hg[i % 2], 16)
                    if i >= 2:
                        y_store(i - 2)
                    if i == 1 and l + 1 < DEPTH:
                        for j in range(1, MOD_MID):
                            mod_store(l + 1, j)
                        mod_columns(l + 1)
                y_store(N_ET - 2)
                y_store(N_ET - 1)
                n0, n1 = (N_ET + 1) // 2, N_ET // 2
                pool.wait_ge(s_yout[0], l * (16 * n0) + 16 * n0)
                pool.wait_ge(s_yout[1], l * (16 * n1) + 16 * n1)
                pool.wait_ge(gu_done, l * N_ET + N_ET)
                for t in range(NT):
                    if t >= 2:
                        pool.wait_ge(x_ready, l * NT + NT + t - 1)
                    for k in range(2):
                        pool.indirect_dma_start(
                            out=y_in[t % 2][k], out_offset=None, in_=y_rows,
                            in_offset=bass.IndirectOffsetOnAxis(ap=slots_i[:, k * NT + t:k * NT + t + 1], axis=0)
                        ).then_inc(s_yin[t % 2], 16)
                if l + 1 < DEPTH:
                    for j in range(MOD_MID, N_MOD):
                        mod_store(l + 1, j)

            dma(gain_b, row_b(a["final_norm_g"], D)).then_inc(s_final, 16)
            for t in range(NT):
                pool.wait_ge(f_ss, t + 1)
                rsqrt(rsf[:, t:t + 1], ssf[:, t:t + 1], 1).then_inc(f_rs, 1)
            for t in range(NT):
                pool.wait_ge(f_out, t + 1)
                dst = o["y_prompt"][0] if t == 0 else o["y_sample"][0, (t - 1) * P:t * P, :]
                dma(dst, x_t[t]).then_inc(s_final, 16)
            pool.wait_ge(s_final, 16 * (NT + 1))
            pool.wait_ge(s_ctxout, DEPTH * 96)

        @block.scalar
        def _(act):
            for k, src in enumerate((a["c_ctx"], a["c"][0])):
                act.dma_start(cond[:, k * KC:(k + 1) * KC], src.rearrange("(p c) -> p c", c=KC)).then_inc(s_cond, 16)
            act.wait_ge(s_cond, 32)
            act.activation(cond_e[:], cond[:], ACT.Exp, scale=-1.0).then_inc(c_e, 1)

            def mod_copy(l, j):
                act.wait_ge(mod_done, l * N_MOD + j + 1)
                if j >= 8:
                    act.wait_ge(s_rowout[0], 64 * (l + 1))
                elif l >= 1:
                    act.wait_ge(s_rowout[j // 4], 64 * l)
                    act.wait_ge(s_rowout[2], 64 * l)
                act.activation(mod_row(j), ps[0:2, 2 + j % 2, :], ACT.Copy).then_inc(mod_evac, 1)

            for j in range(N_MOD):
                mod_copy(0, j)

            for l in range(DEPTH):
                def norm1_sums(t):
                    act.wait_ge(x_ready, l * NT + t + 1)
                    if t >= 2:
                        act.wait_ge(hT_done, l * 2 * NT + 2 * (t - 1))
                    act.activation(xn[t % 2], x_t[t], ACT.Square, scale=D ** -0.5,
                                   accum_out=ss1[:, t:t + 1]).then_inc(ss1_ready, 1)

                def hT_copy(t):
                    act.wait_ge(hT_done, l * 2 * NT + 2 * t + 2)
                    act.wait_ge(a1_ready, l + 1)
                    for q in range(4):
                        c = 4 + q
                        k = min(t, 1)
                        last = act.activation(hT[:, c, t * P:(t + 1) * P], ps[:, 7, q * P:(q + 1) * P],
                                              ACT.Identity, bias=mod_c[:, 0, k, c:c + 1],
                                              scale=mod_c[:, 1, k, c:c + 1])
                    last.then_inc(hT_evac, 1)

                def z_copies(t):
                    act.wait_ge(z_used_d, l * 4 * NT + 4 * t + 1)
                    act.activation(q_tok[t][:, 0:384].rearrange("p (h n) -> p h n", h=HM)[:, :, 0:32],
                                   ps[:, 0, 0:384].rearrange("p (h n) -> p h n", h=HM)[:, :, 0:32],
                                   ACT.Copy).then_inc(z_used_a, 1)
                    act.wait_ge(z_used_d, l * 4 * NT + 4 * t + 3)
                    act.activation(V[:, 2 + t, 384:512], ps[:, 2, 128:256], ACT.Copy).then_inc(z_used_a, 1)
                    act.wait_ge(z_used_d, l * 4 * NT + 4 * t + 4)
                    act.activation(V[:, 2 + t, 512:768], ps[:, 3, 256:512], ACT.Copy).then_inc(z_used_a, 1)

                def key_copies_a(u):
                    act.wait_ge(k1_done, l * NU + u + 1)
                    act.wait_ge(k2_done, l * NU + u + 1)
                    act.activation(ckvT[:], ps[:, 4, 0:128], ACT.Copy)
                    act.activation(kT[:, 3:6, KCOL[u]:KCOL[u] + P],
                                   ps[:, 4, 128:512].rearrange("p (j n) -> p j n", j=3),
                                   ACT.Copy).then_inc(kA_evac, 1)

                def key_copies_b(u):
                    act.wait_ge(k2_done, l * NU + u + 2)
                    act.activation(kT[:, 0:3, KCOL[u]:KCOL[u] + P],
                                   ps[:, 5, 0:384].rearrange("p (j n) -> p j n", j=3), ACT.Copy)
                    act.activation(V[:, u, 0:384], ps[:, 6, 0:384], ACT.Copy).then_inc(kB_evac, 1)

                norm1_sums(0)
                norm1_sums(1)
                hT_copy(0)
                act.wait_ge(x_ready, l * NT + NT)
                for u in range(2):
                    key_copies_a(u)
                    key_copies_b(u)
                for t in range(NT):
                    if t >= 1:
                        key_copies_a(1 + t)
                    if t + 2 < NT:
                        norm1_sums(t + 2)
                    z_copies(t)
                    if t >= 1:
                        key_copies_b(1 + t)
                    if t + 1 < NT:
                        hT_copy(t + 1)
                key_copies_a(NU - 1)
                key_copies_b(NU - 1)

                act.wait_ge(lam_s, l + 1)
                act.activation(lam4[:, 2:4], lam4[:, 0:2], ACT.Exp).then_inc(lam_e, 1)

                def query_copies(gb):
                    b = gb % 8
                    act.wait_ge(qt_done, l * N_Q + gb + 1)
                    src = ps[:, 7, (gb % 2) * P:(gb % 2 + 1) * P]
                    if b < 6:
                        act.activation(pair_q[b % 2][1][64:128, :], src[64:128, :], ACT.Copy).then_inc(qz_a, 1)
                    else:
                        act.activation(quad_q[b % 2][2][64:96, :], src[64:96, :], ACT.Copy)
                        act.activation(quad_q[b % 2][3][96:128, :], src[96:128, :], ACT.Copy).then_inc(qz_a, 1)

                def probs(n):
                    t, h = divmod(n, N_UNIT)
                    act.wait_ge(m_ready, l * N_S + n + 1)
                    if n >= 2:
                        act.wait_ge(pt4_done, l * N_S + n - 1)
                        if n - 2 >= N_UNIT:
                            act.wait_ge(pt5_done, l * N_S5 + n - 1 - N_UNIT)
                    b0 = 2 * (n % 2)
                    col = sums[:, h + N_UNIT * (t % 2):h + N_UNIT * (t % 2) + 1]
                    if t == 0:
                        i_, o_ = ps[:, b0, 0:P], pr[n % 2][:, 0:P]
                    else:
                        i_ = ps[:, b0:b0 + 2, 0:384]
                        o_ = pr[n % 2].rearrange("p (a n) -> p a n", a=2)
                    act.activation(o_, i_, ACT.Exp, bias=negm[:, n % 2:n % 2 + 1], scale=score_map(h)[4],
                                   accum_out=col).then_inc(exp_done, 1)

                def probsT(n):
                    if n < N_UNIT:
                        return
                    act.wait_ge(pt5_done, l * N_S5 + n - N_UNIT + 1)
                    act.wait_ge(pv_done, l * N_S + n - 1)
                    act.activation(prT[n % 2][:, 384:768], ps[:, 5, 0:384], ACT.Copy).then_inc(pt5_evac, 1)

                for n in range(N_S + 1):
                    if n < N_S:
                        h = n % N_UNIT
                        b = score_map(h)[0]
                        if h == MAPS_OF_BLOCK[b][0]:
                            gb = 8 * (n // N_UNIT) + b
                            if gb == 0:
                                query_copies(0)
                            if gb + 1 < N_Q:
                                query_copies(gb + 1)
                    if n >= 1:
                        probsT(n - 1)
                    if n < N_S:
                        probs(n)

                def oT_copy(t):
                    act.wait_ge(oT_done, l * 2 * NT + 2 * t + 2)
                    act.activation(hT[:, 4:8, t * P:(t + 1) * P],
                                   ps[:, 5, :].rearrange("p (c n) -> p c n", c=4), ACT.Copy).then_inc(oT_evac_a, 1)

                def norm2_sums(t):
                    act.wait_ge(xo_done, l * 15 + 3 * t + 3)
                    if t >= 1:
                        act.wait_ge(h2T_done, l * 2 * NT + 2 * t)
                        act.wait_ge(s_hout, l * 80 + 16 * t)
                    act.activation(h2, x_t[t], ACT.Square, scale=D ** -0.5,
                                   accum_out=ss2[:, t:t + 1]).then_inc(ss2_ready, 1)

                def h2T_copy(t):
                    act.wait_ge(h2T_done, l * 2 * NT + 2 * t + 2)
                    if t >= 1:
                        act.wait_ge(rt_done, l * NT + t)
                    act.activation(h2T[:, 4:8, :], ps[:, 7, :].rearrange("p (c n) -> p c n", c=4),
                                   ACT.Copy).then_inc(h2T_evac_a, 1)

                oT_copy(0)
                for t in range(NT):
                    if t + 1 < NT:
                        oT_copy(t + 1)
                    norm2_sums(t)
                    h2T_copy(t)

                act.wait_ge(r_sub, 2 * l + 1)
                act.activation(r_gex, r_gs, ACT.Exp).then_inc(r_exp, 1)
                act.wait_ge(r_sub, 2 * l + 2)
                act.activation(r_ex2, r_d, ACT.Exp).then_inc(r_exp, 1)
                if l + 1 < DEPTH:
                    for j in range(MOD_MID):
                        mod_copy(l + 1, j)

                for i in range(N_ET + 1):
                    if i < N_ET:
                        act.wait_ge(gt_done, l * N_ET + i + 1)
                        if i >= 2:
                            act.wait_ge(gu_done, l * N_ET + i - 1)
                        act.activation(hgT[i % 2][:, 4:8, :], ps[:, 1, :].rearrange("p (c n) -> p c n", c=4),
                                       ACT.Copy).then_inc(gt_evac_a, 1)
                        act.wait_ge(gu_done, l * N_ET + i + 1)
                        if i >= 2:
                            act.wait_ge(hid_ready, l * N_ET + i - 1)
                        act.activation(sig[i % 2], ps[:, 2 + i % 2, 0:FF], ACT.Exp, scale=-1.0
                                       ).then_inc(sig_done, 1)
                    if i >= 1:
                        y_copy_a(act, l, i - 1)
                if l + 1 < DEPTH:
                    for j in range(MOD_MID, N_MOD):
                        mod_copy(l + 1, j)

            for t in range(NT):
                act.wait_ge(x_ready, DEPTH * NT + t + 1)
                act.activation(work[:, 1024 * (t % 2):1024 * (t % 2 + 1)], x_t[t], ACT.Square, scale=D ** -0.5,
                               accum_out=ssf[:, t:t + 1]).then_inc(f_ss, 1)
                act.drain()

        @block.vector
        def _(dve):
            tt, ts, stt, cp = dve.tensor_tensor, dve.tensor_scalar, dve.scalar_tensor_tensor, dve.tensor_copy
            red = dve.tensor_reduce
            dve.wait_ge(c_e, 1)
            ts(cond_e[:], cond_e[:], 1.0, None, ALU.add)
            dve.drain()
            dve.reciprocal(cond_e[:], cond_e[:])
            dve.drain()
            tt(silu_c[:], cond[:], cond_e[:], ALU.mult).then_inc(c_cond, 1)
            dve.wait_ge(c_const, 1)
            dve.wait_ge(s_setup_dma, 64)
            dve.sem_inc(x_ready, NT)
            dve.sem_inc(o_evac, 1)

            for l in range(DEPTH):
                dve.wait_ge(s_modcol, l * 32 + 32)
                dve.wait_ge(s_small, (l + 1) * (16 * N_SMALL_IN))
                for k in range(2):
                    last = stt(mod_c[:, 1, k, :], mod_c[:, 1, k, :], 1.0, n1col[:], ALU.add, ALU.mult)
                last.then_inc(a1_ready, 1)

                def norm_x(t):
                    dve.wait_ge(rs1_ready, l * NT + t + 1)
                    ts(xn[t % 2], x_t[t], rs1[:, t:t + 1], None, ALU.mult).then_inc(xn_ready, 1)

                def hT_copy(t):
                    dve.wait_ge(hT_done, l * 2 * NT + 2 * t + 1)
                    for c in range(4):
                        k = min(t, 1)
                        last = ts(hT[:, c, t * P:(t + 1) * P], ps[:, 7, c * P:(c + 1) * P],
                                  mod_c[:, 1, k, c:c + 1], mod_c[:, 0, k, c:c + 1], ALU.mult, ALU.add)
                    last.then_inc(hT_evac, 1)

                def rotate(t, src, H, w, outs):
                    tab = rope[:, t * 96:(t + 1) * 96]
                    cos, sin = (tab[:, 0:16], tab[:, 16:32]) if w == 16 else (tab[:, 32:64], tab[:, 64:96])
                    n = H * 2 * w
                    C = rope_c[:, 0:n].rearrange("p (h k w) -> p h k w", h=H, k=2)
                    S = rope_s[:, 0:n].rearrange("p (h k w) -> p h k w", h=H, k=2)
                    s4 = src.rearrange("p h (k w) -> p h k w", k=2)
                    tt(C, s4, cos.unsqueeze(1).unsqueeze(1).to_broadcast([P, H, 2, w]), ALU.mult)
                    first = tt(S, s4, sin.unsqueeze(1).unsqueeze(1).to_broadcast([P, H, 2, w]), ALU.mult)
                    dve.drain()
                    for o_ in outs:
                        tt(o_[:, :, 0:w], C[:, :, 0, :], S[:, :, 1, :], ALU.subtract)
                        last = tt(o_[:, :, w:2 * w], S[:, :, 0, :], C[:, :, 1, :], ALU.add)
                    dve.drain()
                    return last

                def z_block(t, b):
                    dve.wait_ge(z_done, l * 4 * NT + 4 * t + b + 1)
                    z = ps[:, b, :]
                    kt = k_view[t % 2]
                    junk = rope_c[:, 0:384]
                    if b == 0:
                        dve.wait_ge(k2_done, l * NU + t + 2)
                        if t == 2:
                            dve.wait_ge(s_ctxout, l * 96 + 96)
                        rotate(t, z[:, 0:384].rearrange("p (h n) -> p h n", h=HM)[:, :, 32:64], HM, 16,
                               [q_tok[t][:, 0:384].rearrange("p (h n) -> p h n", h=HM)[:, :, 32:64]])
                        tt(kt[:, 0:128], z[:, 384:512], kv_g[:], ALU.mult)
                        cp(junk[:, 0:128], z[:, 384:512])
                        dve.drain()
                        tt(junk[:, 0:128], junk[:, 0:128], junk[:, 0:128], ALU.mult).then_inc(z_used_d, 1)
                        dve.drain()
                        red(ss9[:, 0:1], junk[:, 0:128], AX.X, ALU.add)
                        dve.drain()
                    elif b == 1:
                        rotate(t, z[:, 0:32].unsqueeze(1), 1, 16,
                               [kt[:, 160:192].unsqueeze(1), kt[:, 224:256].unsqueeze(1)])
                        qv = z[:, 32:416]
                        cp(junk, qv)
                        qd_ = q_tok[t][:, 384:768]
                        tt(qd_.rearrange("p (j g n) -> p g j n", j=GJ, g=GKV),
                           qv.rearrange("p (g j n) -> p g j n", j=GJ, g=GKV),
                           qn_g[:].unsqueeze(1).unsqueeze(1).to_broadcast([P, GKV, GJ, 64]),
                           ALU.mult).then_inc(z_used_d, 1)
                        dve.drain()
                        tt(junk, junk, junk, ALU.mult)
                        dve.drain()
                        red(ss9[:, 1:7].rearrange("p (j g) -> p g j", j=GJ),
                            junk.rearrange("p (g j n) -> p g j n", j=GJ, g=GKV), AX.X, ALU.add)
                        dve.drain()
                        q3 = qd_.rearrange("p (h n) -> p h n", h=HG)
                        rotate(t, q3, HG, 32, [q3])
                    elif b == 2:
                        kv = z[:, 0:128]
                        cp(junk[:, 0:128], kv)
                        kd_ = kt[:, 256:384]
                        tt(kd_.rearrange("p (g n) -> p g n", g=GKV), kv.rearrange("p (g n) -> p g n", g=GKV),
                           kn_g[:].unsqueeze(1).to_broadcast([P, GKV, 64]), ALU.mult)
                        dve.drain()
                        tt(junk[:, 0:128], junk[:, 0:128], junk[:, 0:128], ALU.mult)
                        dve.drain()
                        red(ss9[:, 7:9], junk[:, 0:128].rearrange("p (g n) -> p g n", g=GKV), AX.X, ALU.add)
                        dve.drain()
                        tt(ss9, ss9, inv9, ALU.mult).then_inc(ss9_ready, 1)
                        k3 = kd_.rearrange("p (g n) -> p g n", g=GKV)
                        rotate(t, k3, GKV, 32, [k3])
                        rotate(t, z[:, 256:512].rearrange("p (h n) -> p h n", h=8), 8, 16,
                               [q_tok[t][:, 768:1024].rearrange("p (h n) -> p h n", h=8)]).then_inc(z_used_d, 1)
                    else:
                        rotate(t, z[:, 0:256].rearrange("p (h n) -> p h n", h=8), 8, 16,
                               [kt[:, 384:640].rearrange("p (h n) -> p h n", h=8)]).then_inc(z_used_d, 1)
                        dve.wait_ge(rs9_ready, l * NT + t + 1)
                        ts(kt[:, 0:128], kt[:, 0:128], rs9[:, 0:1], None, ALU.mult)
                        q3 = q_tok[t][:, 384:768].rearrange("p (h n) -> p h n", h=HG)
                        tt(q3, q3, rs9[:, 1:7].unsqueeze(2).to_broadcast([P, HG, 64]), ALU.mult)
                        k3 = kt[:, 256:384].rearrange("p (g n) -> p g n", g=GKV)
                        tt(k3, k3, rs9[:, 7:9].unsqueeze(2).to_broadcast([P, GKV, 64]),
                           ALU.mult)
                        dve.drain()
                        dve.sem_inc(k_ready, 1)

                norm_x(0)
                hT_copy(0)
                for t in range(NT):
                    if t + 1 < NT:
                        norm_x(t + 1)
                    z_block(t, 0)
                    z_block(t, 1)
                    z_block(t, 2)
                    if t + 1 < NT:
                        hT_copy(t + 1)
                    z_block(t, 3)

                lp = lam_in[:].rearrange("p (a k n) -> p a k n", a=2, k=2)
                lw = rope_c[:, 0:64].rearrange("p (a n) -> p a n", a=2)
                tt(lw, lp[:, :, 0, :], lp[:, :, 1, :], ALU.mult)
                dve.drain()
                red(lam4[:, 0:2], lw, AX.X, ALU.add).then_inc(lam_s, 1)
                dve.wait_ge(lam_e, l + 1)
                tt(lam, lam4[:, 2:3], lam4[:, 3:4], ALU.subtract)
                ts(df_g[:], df_g[:], lconst[:, 1:2], None, ALU.mult)
                dve.drain()
                tt(lam, lam, lconst[:, 0:1], ALU.add)
                dve.drain()

                def query_copies(gb):
                    b = gb % 8
                    dve.wait_ge(qt_done, l * N_Q + gb + 1)
                    src = ps[:, 7, (gb % 2) * P:(gb % 2 + 1) * P]
                    if b < 6:
                        cp(pair_q[b % 2][0][0:64, :], src[0:64, :]).then_inc(qz_d, 1)
                    else:
                        cp(quad_q[b % 2][0][0:32, :], src[0:32, :])
                        cp(quad_q[b % 2][1][32:64, :], src[32:64, :]).then_inc(qz_d, 1)

                def row_max(n):
                    t, h = divmod(n, N_UNIT)
                    dve.wait_ge(s_done, l * N_S + n + 1)
                    b0 = 2 * (n % 2)
                    if t == 0:
                        red(mx[:, n % 2:n % 2 + 1], ps[:, b0, 0:P], AX.X, ALU.max)
                    else:
                        red(mx[:, n % 2:n % 2 + 1], ps[:, b0:b0 + 2, 0:384], AX.XY, ALU.max)
                    dve.drain()
                    if n >= 2:
                        dve.wait_ge(exp_done, l * N_S + n - 1)
                    ts(negm[:, n % 2:n % 2 + 1], mx[:, n % 2:n % 2 + 1], -score_map(h)[4], None,
                       ALU.mult).then_inc(m_ready, 1)

                def probsT(n):
                    dve.wait_ge(pt4_done, l * N_S + n + 1)
                    if n >= 2:
                        dve.wait_ge(pv_done, l * N_S + n - 1)
                    w = P if n < N_UNIT else 384
                    cp(prT[n % 2][:, 0:w], ps[:, 4, 0:w]).then_inc(pt4_evac, 1)

                def head_out(n):
                    t, h = divmod(n, N_UNIT)
                    c = out_column(h)
                    m = h - HM - HG
                    col = sums[:, h + N_UNIT * (t % 2):h + N_UNIT * (t % 2) + 1]
                    r = rec[:, n % 2:n % 2 + 1]
                    dve.wait_ge(pv_done, l * N_S + n + 1)
                    dve.reciprocal(r, col)
                    dve.drain()
                    O = ps[:, 6, (n % 2) * 64:(n % 2 + 1) * 64]
                    dst = q_tok[t][:, c:c + 64]
                    if m >= 0 and m % 2 == 1:
                        stt(r, r, -1.0, lam, ALU.mult, ALU.mult)
                        dve.drain()
                        stt(dst, O, r, dst, ALU.mult, ALU.add).then_inc(o_evac, 1)
                        dve.drain()
                    else:
                        ts(dst, O, r, None, ALU.mult).then_inc(o_evac, 1)
                        if m >= 0:
                            dve.drain()

                def diff_sums(t):
                    od = q_tok[t][:, 768:1024]
                    sq = k_tok[:, 256:512]
                    tt(sq, od, od, ALU.mult)
                    dve.drain()
                    red(ss4, sq.rearrange("p (h n) -> p h n", h=HD), AX.X, ALU.add)
                    dve.drain()
                    ts(ss4, ss4, 1.0 / 64, None, ALU.mult).then_inc(ss4_ready, 1)

                def diff_norm(t):
                    od = q_tok[t][:, 768:1024].rearrange("p (h n) -> p h n", h=HD)
                    dve.wait_ge(rs4_ready, l * NT + t + 1)
                    tt(od, od, rs4.unsqueeze(2).to_broadcast([P, HD, 64]), ALU.mult)
                    dve.drain()
                    tt(od, od, df_g[:].unsqueeze(1).to_broadcast([P, HD, 64]), ALU.mult).then_inc(o_ready, 1)

                for n in range(N_S + 2):
                    if n < N_S:
                        h = n % N_UNIT
                        b = score_map(h)[0]
                        if h == MAPS_OF_BLOCK[b][0]:
                            gb = 8 * (n // N_UNIT) + b
                            if gb == 0:
                                query_copies(0)
                            if gb + 1 < N_Q:
                                query_copies(gb + 1)
                        row_max(n)
                    if 1 <= n <= N_S:
                        probsT(n - 1)
                    if n >= 2:
                        head_out(n - 2)
                        if (n - 2) % N_UNIT == N_UNIT - 1:
                            diff_sums((n - 2) // N_UNIT)
                    if n >= 4 and (n - 4) % N_UNIT == N_UNIT - 1:
                        diff_norm((n - 4) // N_UNIT)
                diff_norm(NT - 1)

                def oT_copy(t):
                    dve.wait_ge(oT_done, l * 2 * NT + 2 * t + 1)
                    cp(hT[:, 0:4, t * P:(t + 1) * P],
                       ps[:, 4, :].rearrange("p (c n) -> p c n", c=4)).then_inc(oT_evac_d, 1)

                def x_add(t, b):
                    c0, c1 = WO_COLS[b]
                    n = 3 * t + b
                    if n == 0:
                        dve.wait_ge(s_gate1, (l + 1) * 32)
                    dve.wait_ge(wo_done, l * 15 + n + 1)
                    tt(xo_tmp[:, 0:c1 - c0], ps[:, n % 4, 0:c1 - c0], (gate1l if t else gate1c)[:, c0:c1], ALU.mult)
                    dve.drain()
                    tt(x_t[t][:, c0:c1], x_t[t][:, c0:c1], xo_tmp[:, 0:c1 - c0], ALU.add).then_inc(xo_done, 1)
                    dve.drain()

                def mixer_in(t):
                    k = min(t, 1)
                    if t == 0:
                        dve.wait_ge(s_bcast, (l + 1) * (16 * 7))
                        for q in range(2):
                            stt(a2b[:, q, :], a2b[:, q, :], 1.0, gain_b, ALU.add, ALU.mult)
                        dve.drain()
                    dve.wait_ge(rs2_ready, l * NT + t + 1)
                    stt(h2, x_t[t], rs2[:, t:t + 1], a2b[:, k, :], ALU.mult, ALU.mult)
                    dve.drain()
                    tt(h2, h2, b2b[:, k, :], ALU.add).then_inc(h2_ready, 1)

                def h2T_copy(t):
                    dve.wait_ge(h2T_done, l * 2 * NT + 2 * t + 1)
                    if t >= 1:
                        dve.wait_ge(rt_done, l * NT + t)
                    cp(h2T[:, 0:4, :], ps[:, 6, :].rearrange("p (c n) -> p c n", c=4)).then_inc(h2T_evac_d, 1)

                def logits_in(t):
                    dve.wait_ge(rt_done, l * NT + t + 1)
                    tt(logits[:, t, :], ps[:, 6, 0:20], b_rt[:], ALU.add).then_inc(lg_ready, 1)

                oT_copy(0)
                for t in range(NT):
                    x_add(t, 0)
                    if t >= 1:
                        h2T_copy(t - 1)
                    if t + 1 < NT:
                        oT_copy(t + 1)
                    x_add(t, 1)
                    if t >= 1:
                        logits_in(t - 1)
                    x_add(t, 2)
                    mixer_in(t)
                h2T_copy(NT - 1)
                logits_in(NT - 1)
                dve.drain()

                dve.wait_ge(s_hout, l * 80 + 80)
                G, E = logits[:, :, 0:4], logits[:, :, 4:20]

                def bc(v, n):
                    return v.unsqueeze(2).to_broadcast([P, NT, n])

                def first_of(vals, top, out):
                    tt(v3(r_t1, 4), vals, bc(top, 4), ALU.is_equal)
                    dve.drain()
                    tt(v3(r_t2, 4), v3(r_t1, 4), desc[:].unsqueeze(1).to_broadcast([P, NT, 4]), ALU.mult)
                    dve.drain()
                    red(r_t3, v3(r_t2, 4), AX.X, ALU.max)
                    dve.drain()
                    tt(v3(out, 4), v3(r_t2, 4), bc(r_t3, 4), ALU.is_equal)
                    dve.drain()

                red(r_gm, G, AX.X, ALU.max)
                dve.drain()
                tt(v3(r_gs, 4), G, bc(r_gm, 4), ALU.subtract).then_inc(r_sub, 1)
                first_of(G, r_gm, r_og)
                tt(v4(r_sel), E.rearrange("p t (g e) -> p t g e", g=NGRP),
                   v3(r_og, 4).unsqueeze(3).to_broadcast([P, NT, NGRP, EPG]), ALU.mult)
                dve.drain()
                red(v3(r_es, 4), r_sel.rearrange("p (t g e) -> p t e g", t=NT, g=NGRP), AX.X, ALU.add)
                dve.drain()
                red(r_m1, v3(r_es, 4), AX.X, ALU.max)
                dve.drain()
                first_of(v3(r_es, 4), r_m1, r_o1)
                stt(r_es2, r_o1, -3.0e38, r_es, ALU.mult, ALU.add)
                dve.drain()
                red(r_m2, v3(r_es2, 4), AX.X, ALU.max)
                dve.drain()
                tt(r_d, r_m2, r_m1, ALU.subtract).then_inc(r_sub, 1)
                first_of(v3(r_es2, 4), r_m2, r_o2)
                for O_, o_ in ((r_O1, r_o1), (r_O2, r_o2)):
                    tt(v4(O_), v3(r_og, 4).unsqueeze(3).to_broadcast([P, NT, NGRP, EPG]),
                       v3(o_, 4).unsqueeze(2).to_broadcast([P, NT, NGRP, EPG]), ALU.mult)
                dve.drain()
                tt(r_M, r_O1, r_O2, ALU.add).then_inc(r_mask, 1)
                dve.wait_ge(r_exp, 2 * l + 2)
                red(r_gtop, v3(r_gex, 4), AX.X, ALU.add)
                ts(r_den, r_ex2, 1.0, None, ALU.add)
                dve.drain()
                tt(r_den, r_den, r_gtop, ALU.mult)
                dve.drain()
                dve.reciprocal(rout_w[:, 0:NT], r_den)
                dve.drain()
                tt(rout_w[:, NT:2 * NT], rout_w[:, 0:NT], r_ex2, ALU.mult)
                dve.wait_ge(r_count, l + 1)
                cp(r_cn, ps[:, 6, 128:208])
                cp(r_rank, ps[:, 6, 256:336])
                dve.drain()
                big4 = r_big.rearrange("p (t e s) -> p t e s", t=NT, e=NE)
                tt(big4, r_cn.rearrange("p (s e) -> p e s", e=NE).unsqueeze(1).to_broadcast([P, NT, NE, NT]),
                   v3(lt[:], NT).unsqueeze(2).to_broadcast([P, NT, NE, NT]), ALU.mult)
                red(r_c, r_cn.rearrange("p (s e) -> p e s", e=NE), AX.X, ALU.add)
                dve.drain()
                red(v3(r_add, NE), big4, AX.X, ALU.add)
                dve.drain()
                tt(r_rank, r_rank, r_add, ALU.add)
                b3 = r_big[:, 0:NE * NT].rearrange("p (e s) -> p e s", e=NE)
                tt(b3, r_c.unsqueeze(2).to_broadcast([P, NE, NT]),
                   k128[:].unsqueeze(1).to_broadcast([P, NE, NT]), ALU.is_gt)
                dve.drain()
                red(r_nt, b3, AX.X, ALU.add)
                dve.drain()
                b5 = r_big[:, 0:NE * NE].rearrange("p (e s) -> p e s", e=NE)
                tt(b5, r_nt.unsqueeze(1).to_broadcast([P, NE, NE]),
                   le[:].rearrange("p (e s) -> p e s", e=NE), ALU.mult)
                dve.drain()
                red(r_incl, b5, AX.X, ALU.add)
                dve.drain()
                b6 = r_big[0:1, 0:N_ET * NE].rearrange("p (i e) -> p i e", e=NE)
                tt(b6, r_incl[0:1, :].unsqueeze(1).to_broadcast([1, N_ET, NE]),
                   iota_t[0:1, :].unsqueeze(2).to_broadcast([1, N_ET, NE]), ALU.is_le)
                tt(r_excl, r_incl, r_nt, ALU.subtract)
                dve.drain()
                red(r_ex[0:1, :], b6, AX.X, ALU.add)
                stt(v3(r_rank, NE), r_excl.unsqueeze(1).to_broadcast([P, NT, NE]), float(P), v3(r_rank, NE),
                    ALU.mult, ALU.add)
                dve.drain()
                ts(experts_i[0:1, :], r_ex[0:1, :], float(NE - 1), None, ALU.min).then_inc(experts_ready, 1)
                tt(r_O1, r_O1, r_rank, ALU.mult)
                tt(r_O2, r_O2, r_rank, ALU.mult)
                dve.drain()
                red(r_sl[:, 0:NT], v3(r_O1, NE), AX.X, ALU.add)
                red(r_sl[:, NT:2 * NT], v3(r_O2, NE), AX.X, ALU.add)
                dve.drain()
                cp(slots_i[:], r_sl).then_inc(slots_ready, 1)

                def rows_in(i):
                    dve.wait_ge(gt_done, l * N_ET + i + 1)
                    if i >= 2:
                        dve.wait_ge(gu_done, l * N_ET + i - 1)
                    cp(hgT[i % 2][:, 0:4, :], ps[:, 0, :].rearrange("p (c n) -> p c n", c=4)).then_inc(gt_evac_d, 1)

                def hidden(i):
                    G_ = ps[:, 2 + i % 2, :]
                    dve.wait_ge(sig_done, l * N_ET + i + 1)
                    ts(sig[i % 2], sig[i % 2], 1.0, None, ALU.add)
                    dve.drain()
                    dve.reciprocal(sig[i % 2], sig[i % 2])
                    dve.drain()
                    tt(sig[i % 2], sig[i % 2], G_[:, 0:FF], ALU.mult)
                    dve.drain()
                    if i >= 2:
                        dve.wait_ge(ht_done, l * N_ET + i - 1)
                    tt(hid[i % 2], sig[i % 2], G_[:, FF:2 * FF], ALU.mult).then_inc(hid_ready, 1)

                def hiddenT(i):
                    dve.wait_ge(ht_done, l * N_ET + i + 1)
                    if i >= 2:
                        dve.wait_ge(dn_done, l * N_ET + i - 1)
                    cp(hidT[i % 2], ps[:, 4, 0:FF].rearrange("p (c n) -> p c n", c=2)).then_inc(ht_evac, 1)

                def y_copy(i):
                    dve.wait_ge(dn_done, l * N_ET + i + 1)
                    y_buffer_free(dve, l, i)
                    cp(y_out[i % 2][:, 0:512], ps[:, 5, :]).then_inc(y_evac_d, 1)

                rows_in(0)
                for i in range(N_ET + 1):
                    if i >= 1:
                        hiddenT(i - 1)
                    if i < N_ET:
                        hidden(i)
                    if i >= 1:
                        y_copy(i - 1)
                    if i + 1 < N_ET:
                        rows_in(i + 1)

                for t in range(NT):
                    n = (3, 2)[t % 2]
                    dve.wait_ge(s_yin[t % 2], l * (32 * n) + 32 * (t // 2 + 1))
                    y1, y2 = y_in[t % 2]
                    ts(y1, y1, rout_w[:, t:t + 1], None, ALU.mult)
                    dve.drain()
                    stt(y1, y2, rout_w[:, NT + t:NT + t + 1], y1, ALU.mult, ALU.add)
                    dve.drain()
                    tt(y1, y1, gate2b[:, min(t, 1), :], ALU.mult)
                    dve.drain()
                    tt(x_t[t], x_t[t], y1, ALU.add).then_inc(x_ready, 1)
                    dve.drain()

            dve.wait_ge(s_final, 16)
            for t in range(NT):
                dve.wait_ge(f_rs, t + 1)
                stt(x_t[t], x_t[t], rsf[:, t:t + 1], gain_b, ALU.mult, ALU.mult).then_inc(f_out, 1)

        @block.tensor
        def _(pe):
            mm = pe.matmul

            def tr(out, in_):
                return pe.transpose(out, in_, ident[:])
            pe.sem_inc(k2_done, 1)
            pe.sem_inc(hT_evac, 1)
            pe.sem_inc(kA_evac, 1)
            pe.sem_inc(kB_evac, 1)
            pe.wait_ge(c_cond, 1)

            def mod_chunk(l, j):
                g = USE_AT["mod", l, j]
                pe.wait_ge(w_landed[g % RING], USE_CUM[g])
                if l * N_MOD + j >= 1:
                    pe.wait_ge(mod_evac, max(l * N_MOD + j - 1, 1))
                w = slot[g % RING].rearrange("p (c n) -> p c n", c=KC)
                for c in range(KC):
                    last = mm(ps[0:2, 2 + j % 2, :], silu_v[:, :, c], w[:, c, :],
                              start=(c == 0), stop=(c == KC - 1))
                last.then_inc(mod_done, 1)

            for j in range(N_MOD):
                mod_chunk(0, j)
            pe.wait_ge(c_const, 1)

            for l in range(DEPTH):
                w_slots = {}

                def landed(kind, i):
                    g = USE_AT[kind, l, i]
                    pe.wait_ge(w_landed[g % RING], USE_CUM[g])
                    return slot[g % RING]

                def hT_round(t, r):
                    pe.wait_ge(xn_ready, l * NT + t + 1)
                    pe.wait_ge(hT_evac, l * 2 * NT + 2 * t + r + 1)
                    for q in range(4):
                        last = tr(ps[:, 7, q * P:(q + 1) * P], xn[t % 2][:, 4 * r + q:D:KC])
                    last.then_inc(hT_done, 1)

                def z_block(t, b):
                    if t == 0:
                        w_slots["in", b] = landed("in", b)
                        if b == 0:
                            pe.wait_ge(mod_evac, (l + 1) * N_MOD)
                        pe.wait_ge(hT_evac, l * 2 * NT + 3)
                    else:
                        pe.wait_ge(z_used_d, l * 4 * NT + 4 * (t - 1) + b + 1)
                        if b != 1:
                            pe.wait_ge(z_used_a, l * 3 * NT + 3 * (t - 1) + (1, 0, 2, 3)[b])
                        pe.wait_ge(hT_evac, l * 2 * NT + 2 * t + 3)
                    n = BLK[b][1] - BLK[b][0]
                    w = w_slots["in", b][:, 0:KC * n].rearrange("p (c n) -> p c n", c=KC)
                    for c in range(KC):
                        last = mm(ps[:, b, 0:n], hT[:, c, t * P:(t + 1) * P], w[:, c, :],
                                  start=(c == 0), stop=(c == KC - 1))
                    last.then_inc(z_done, 1)

                def keys1(u):
                    kt = k_view[u % 2]
                    if u < 2:
                        pe.wait_ge(s_small, (l + 1) * (16 * N_SMALL_IN))
                    else:
                        pe.wait_ge(k_ready, l * NT + u - 1)
                    pe.wait_ge(kA_evac, l * NU + u + 1)
                    tr(ps[:, 4, 0:128], kt[:, 0:128])
                    tr(ps[:, 4, 128:256], kt[:, 256:384])
                    tr(ps[:, 4, 256:384], kt[:, 384:512])
                    tr(ps[:, 4, 384:512], kt[:, 512:640]).then_inc(k1_done, 1)

                def keys2(u):
                    kt = k_view[u % 2]
                    pe.wait_ge(kA_evac, l * NU + u + 2)
                    pe.wait_ge(kB_evac, l * NU + u + 1)
                    for j in range(3):
                        mm(ps[:, 5, j * P:(j + 1) * P], wuk[:, j * P:(j + 1) * P], ckvT[:], start=True, stop=False)
                        mm(ps[:, 5, j * P:(j + 1) * P], kt[:, 128:256], ident[:], start=False, stop=True)
                    mm(ps[:, 6, 0:384], ckvT[:], wuv[:], start=True, stop=True).then_inc(k2_done, 1)

                hT_round(0, 0)
                hT_round(0, 1)
                for u in range(2):
                    keys1(u)
                    keys2(u)
                for t in range(NT):
                    z_block(t, 0)
                    if t >= 1:
                        keys1(1 + t)
                    z_block(t, 1)
                    z_block(t, 2)
                    if t >= 1:
                        keys2(1 + t)
                    if t + 1 < NT:
                        hT_round(t + 1, 0)
                    z_block(t, 3)
                    if t + 1 < NT:
                        hT_round(t + 1, 1)
                keys1(NU - 1)
                keys2(NU - 1)

                def query_block(gb):
                    t, b = divmod(gb, 8)
                    if gb == 0:
                        pe.wait_ge(k_ready, l * NT + NT)
                        pe.wait_ge(z_used_a, (l + 1) * (3 * NT))
                        pe.wait_ge(hT_evac, (l + 1) * (2 * NT) + 1)
                    if gb >= 1:
                        pe.wait_ge(qz_d, l * N_Q + gb)
                        pe.wait_ge(qz_a, l * N_Q + gb)
                    tr(ps[:, 7, (gb % 2) * P:(gb % 2 + 1) * P],
                       q_tok[t][:, b * P:(b + 1) * P]).then_inc(qt_done, 1)

                def scores(n):
                    t, h = divmod(n, N_UNIT)
                    b, part, plane, _, _ = score_map(h)
                    if n == 0:
                        pe.wait_ge(kB_evac, (l + 1) * NU + 1)
                        pe.wait_ge(z_used_d, (l + 1) * (4 * NT))
                    pe.wait_ge(qz_d, l * N_Q + 8 * t + b + 1)
                    pe.wait_ge(qz_a, l * N_Q + 8 * t + b + 1)
                    if n >= 2:
                        pe.wait_ge(exp_done, l * N_S + n - 1)
                    q = (pair_q if b < 6 else quad_q)[b % 2][part]
                    b0 = 2 * (n % 2)
                    if t == 0:
                        mm(ps[:, b0, 0:P], q, kT[:, plane, 768:896], start=True, stop=True).then_inc(s_done, 1)
                    else:
                        mm(ps[:, b0, 0:384], q, kT[:, plane, 0:384], start=True, stop=True)
                        mm(ps[:, b0 + 1, 0:384], q, kT[:, plane, 384:768], start=True, stop=True).then_inc(s_done, 1)

                def probsT(n):
                    pe.wait_ge(exp_done, l * N_S + n + 1)
                    if n >= 1:
                        pe.wait_ge(pt4_evac, l * N_S + n)
                    else:
                        pe.wait_ge(kA_evac, (l + 1) * NU + 1)
                    if n < N_UNIT:
                        tr(ps[:, 4, 0:P], pr[n % 2][:, 0:P]).then_inc(pt4_done, 1)
                        return
                    for c in range(3):
                        last = tr(ps[:, 4, c * P:(c + 1) * P], pr[n % 2][:, c * P:(c + 1) * P])
                    last.then_inc(pt4_done, 1)
                    if n > N_UNIT:
                        pe.wait_ge(pt5_evac, l * N_S5 + n - N_UNIT)
                    for c in range(3):
                        last = tr(ps[:, 5, c * P:(c + 1) * P], pr[n % 2][:, (3 + c) * P:(4 + c) * P])
                    last.then_inc(pt5_done, 1)

                def values(n):
                    t, h = divmod(n, N_UNIT)
                    vc = score_map(h)[3]
                    pe.wait_ge(pt4_evac, l * N_S + n + 1)
                    if t >= 1:
                        pe.wait_ge(pt5_evac, l * N_S5 + n - N_UNIT + 1)
                    pe.wait_ge(o_evac, l * N_S + n + 1)
                    units = [2] if t == 0 else SEEN
                    for c, u in enumerate(units):
                        last = mm(ps[:, 6, (n % 2) * 64:(n % 2 + 1) * 64], prT[n % 2][:, c * P:(c + 1) * P],
                                  V[:, u, vc:vc + 64], start=(c == 0), stop=(c == len(units) - 1))
                    last.then_inc(pv_done, 1)

                for n in range(N_S + 2):
                    if n < N_S:
                        h = n % N_UNIT
                        b = score_map(h)[0]
                        if h == MAPS_OF_BLOCK[b][0]:
                            gb = 8 * (n // N_UNIT) + b
                            if gb == 0:
                                query_block(0)
                            if gb + 1 < N_Q:
                                query_block(gb + 1)
                        scores(n)
                    if 1 <= n <= N_S:
                        probsT(n - 1)
                    if n >= 2:
                        values(n - 2)

                def oT_round(t, r):
                    pe.wait_ge(o_ready, l * NT + t + 1)
                    if t >= 1:
                        pe.wait_ge((oT_evac_d, oT_evac_a)[r], l * NT + t)
                    else:
                        pe.wait_ge(pt4_evac, l * N_S + N_S)
                        pe.wait_ge(pt5_evac, l * N_S5 + N_S5)
                    for q in range(4):
                        last = tr(ps[:, 4 + r, q * P:(q + 1) * P], q_tok[t][:, 4 * r + q:D:KC])
                    last.then_inc(oT_done, 1)

                def out_block(t, b):
                    n = 3 * t + b
                    if t == 0:
                        w_slots["out", b] = landed("out", b)
                    if n >= 4:
                        pe.wait_ge(xo_done, l * 15 + n - 3)
                    else:
                        pe.wait_ge(exp_done, (l + 1) * N_S)
                    pe.wait_ge(oT_evac_d, l * NT + t + 1)
                    pe.wait_ge(oT_evac_a, l * NT + t + 1)
                    w_ = WO_COLS[b][1] - WO_COLS[b][0]
                    w = w_slots["out", b][:, 0:KC * w_].rearrange("p (c n) -> p c n", c=KC)
                    for c in range(KC):
                        last = mm(ps[:, n % 4, 0:w_], hT[:, c, t * P:(t + 1) * P], w[:, c, :],
                                  start=(c == 0), stop=(c == KC - 1))
                    last.then_inc(wo_done, 1)

                def h2T_rounds(t):
                    pe.wait_ge(h2_ready, l * NT + t + 1)
                    if t == 0:
                        pe.wait_ge(o_evac, (l + 1) * N_S + 1)
                        pe.wait_ge(qz_d, (l + 1) * N_Q)
                        pe.wait_ge(qz_a, (l + 1) * N_Q)
                    else:
                        pe.wait_ge(lg_ready, l * NT + t)
                        pe.wait_ge(h2T_evac_a, l * NT + t)
                    for r in range(2):
                        for q in range(4):
                            last = tr(ps[:, 6 + r, q * P:(q + 1) * P], h2[:, 4 * r + q:D:KC])
                        last.then_inc(h2T_done, 1)

                def router(t):
                    pe.wait_ge(h2T_evac_d, l * NT + t + 1)
                    pe.wait_ge(h2T_evac_a, l * NT + t + 1)
                    w = w_rt[:].rearrange("p (c n) -> p c n", c=KC)
                    for c in range(KC):
                        last = mm(ps[:, 6, 0:20], h2T[:, c, :], w[:, c, :], start=(c == 0), stop=(c == KC - 1))
                    last.then_inc(rt_done, 1)

                oT_round(0, 0)
                oT_round(0, 1)
                for t in range(NT):
                    out_block(t, 0)
                    if t + 1 < NT:
                        oT_round(t + 1, 0)
                    if t >= 1:
                        h2T_rounds(t - 1)
                    out_block(t, 1)
                    if t + 1 < NT:
                        oT_round(t + 1, 1)
                    if t >= 1:
                        router(t - 1)
                    out_block(t, 2)
                h2T_rounds(NT - 1)
                router(NT - 1)
                pe.wait_ge(xo_done, l * 15 + 15)
                if l + 1 < DEPTH:
                    mod_chunk(l + 1, 0)
                pe.wait_ge(r_mask, l + 1)
                pe.wait_ge(lg_ready, l * NT + NT)
                mm(ps[:, 6, 128:208], ones[:], r_M, start=True, stop=True)
                mm(ps[:, 6, 256:336], tri[:], r_M, start=True, stop=True).then_inc(r_count, 1)

                def rows_T(i):
                    n = ((N_ET + 1) // 2, N_ET // 2)[i % 2]
                    pe.wait_ge(s_hg[i % 2], l * (16 * n) + 16 * (i // 2 + 1))
                    if i >= 1:
                        pe.wait_ge(gt_evac_d, l * N_ET + i)
                        pe.wait_ge(gt_evac_a, l * N_ET + i)
                    else:
                        pe.wait_ge(xo_done, l * 15 + 15)
                    for c in range(KC):
                        last = tr(ps[:, c // 4, (c % 4) * P:(c % 4 + 1) * P], hg[i % 2][:, c:D:KC])
                    last.then_inc(gt_done, 1)

                def gate_up(i):
                    w = landed("moe", i).rearrange("p (c n) -> p c n", c=KC)
                    pe.wait_ge(gt_evac_d, l * N_ET + i + 1)
                    pe.wait_ge(gt_evac_a, l * N_ET + i + 1)
                    if i >= 2:
                        pe.wait_ge(hid_ready, l * N_ET + i - 1)
                    elif l + 1 < DEPTH:
                        pe.wait_ge(mod_evac, (l + 1) * N_MOD + MOD_MID)
                    for c in range(KC):
                        last = mm(ps[:, 2 + i % 2, :], hgT[i % 2][:, c, :], w[:, c, :],
                                  start=(c == 0), stop=(c == KC - 1))
                    last.then_inc(gu_done, 1)

                def hidden_T(i):
                    pe.wait_ge(hid_ready, l * N_ET + i + 1)
                    if i >= 1:
                        pe.wait_ge(ht_evac, l * N_ET + i)
                    for c in range(2):
                        last = tr(ps[:, 4, c * P:(c + 1) * P], hid[i % 2][:, c:FF:2])
                    last.then_inc(ht_done, 1)

                def down(i):
                    n = ((N_ET + 1) // 2, N_ET // 2)[i % 2]
                    pe.wait_ge(wd_landed[i % 2], l * (16 * n) + 16 * (i // 2 + 1))
                    pe.wait_ge(ht_evac, l * N_ET + i + 1)
                    if i >= 1:
                        pe.wait_ge(y_evac_d, l * N_ET + i)
                        pe.wait_ge(y_evac_a, l * N_ET + i)
                    w = w_dn[i % 2].rearrange("p (c n) -> p c n", c=2)
                    for k in range(2):
                        for c in range(2):
                            last = mm(ps[:, 5 + k, :], hidT[i % 2][:, c, :], w[:, c, k * 512:(k + 1) * 512],
                                      start=(c == 0), stop=(c == 1))
                    last.then_inc(dn_done, 1)

                if l + 1 < DEPTH:
                    for j in range(1, MOD_MID):
                        mod_chunk(l + 1, j)
                rows_T(0)
                for i in range(N_ET + 1):
                    if i >= 1:
                        hidden_T(i - 1)
                    if i < N_ET:
                        gate_up(i)
                    if i >= 1:
                        down(i - 1)
                    if i + 1 < N_ET:
                        rows_T(i + 1)
                if l + 1 < DEPTH:
                    for j in range(MOD_MID, N_MOD):
                        mod_chunk(l + 1, j)


_INS = ['x_prompt', 'x_sample', 'c', 'cache_mla_ckv', 'cache_mla_krope', 'cache_gqa_k', 'cache_gqa_v',
        'cache_diff_k', 'cache_diff_v', 'c_ctx', 'norm1_g', 'norm2_g', 'w_mod', 'b_mod', 'w_in',
        'mla_kv_norm_g', 'mla_w_uk', 'mla_w_uv', 'gqa_q_norm_g', 'gqa_k_norm_g', 'diff_lambda', 'diff_norm_g',
        'w_out', 'moe_w_group', 'moe_b_group', 'moe_w_router', 'moe_b_router', 'moe_w_gate', 'moe_w_up',
        'moe_w_down', 'final_norm_g']

_OUTS = [('y_prompt', (1, T_CTX, D)), ('y_sample', (1, T_LAT, D)),
         ('new_mla_ckv', (1, DEPTH, T_CTX, RANK)), ('new_mla_krope', (1, DEPTH, T_CTX, 32)),
         ('new_gqa_k', (1, DEPTH, T_CTX, GKV, 64)), ('new_gqa_v', (1, DEPTH, T_CTX, GKV, 64)),
         ('new_diff_k', (1, DEPTH, T_CTX, HD, 2, 32)), ('new_diff_v', (1, DEPTH, T_CTX, HD, 64))]


def _rope_table():
    tab = np.zeros((NT * P, 96), np.float32)
    tab[:, 0:16] = 1.0
    tab[:, 32:64] = 1.0
    n = np.arange(T_LAT)
    row, col = (n // GRID_W).astype(np.float32), (n % GRID_W).astype(np.float32)
    for rot, c0 in ((32, 0), (64, 32)):
        quarter = rot // 4
        inv = (np.float32(ROPE_THETA) ** (-np.arange(quarter, dtype=np.float32) / np.float32(quarter))).astype(np.float32)
        ang = np.concatenate([row[:, None] * inv, col[:, None] * inv], axis=-1)
        tab[T_CTX:, c0:c0 + rot // 2] = np.cos(ang)
        tab[T_CTX:, c0 + rot // 2:c0 + rot] = np.sin(ang)
    return tab


def _layer_consts():
    out = np.zeros((DEPTH, 8), np.float32)
    for i in range(DEPTH):
        lam_init = 0.8 - 0.6 * float(np.exp(-0.3 * i))
        out[i, 0], out[i, 1] = lam_init, 1.0 - lam_init
    return out


def kernel(**inputs):
    import concourse.bacc as _bacc
    from concourse.bass_utils import run_bass_kernel_spmd as _run

    nc = _bacc.Bacc("TRN2", target_bir_lowering=False, num_devices=1)
    arrays, a, o = {}, {}, {}
    given = {name: np.ascontiguousarray(inputs[name]) for name in _INS}
    given["rope_table"] = _rope_table()
    given["layer_consts"] = _layer_consts()
    for name, v in given.items():
        arrays[f"in_{name}"] = v
        a[name] = nc.dram_tensor(f"in_{name}", v.shape, mybir.dt.from_np(v.dtype), kind="ExternalInput").ap()
    for name, shape in _OUTS:
        o[name] = nc.dram_tensor(f"out_{name}", shape, F32, kind="ExternalOutput").ap()
    trunk(nc, a, o)
    r = _run(nc, [arrays], core_ids=[0])
    return tuple(r.results[0][f"out_{name}"] for name, _ in _OUTS)
```

```python
from contextlib import ExitStack, nullcontext

import numpy as np
import concourse.bass as bass
from concourse import mybir

F32 = mybir.dt.float32
I32 = mybir.dt.int32
ALU = mybir.AluOpType
ACT = mybir.ActivationFunctionType
AX = mybir.AxisListType

P = 128
D = 1024
KC = D // P
DEPTH = 2
T_CTX, T_LAT, PAST = 128, 512, 256
NT = (T_CTX + T_LAT) // P
EPS = 1e-6
GRID_W = 64
ROPE_THETA = 10000.0
RANK = 128
HM, HG, GKV, GJ, HD = 6, 6, 2, 3, 4
FF = 256
NE, NGRP, EPG = 16, 4, 4
BLK = [(0, 512), (512, 928), (928, 1440), (1440, 1952)]
N_PAIR = 2 * NT * P
N_ET = (N_PAIR + NE * (P - 1)) // P
N_SLOT = N_ET * P
MIN_ET = -(-N_PAIR // P)
N_SMALL_IN = 18

NU = 2 + NT
KCOL = [0, 128, 768, 256, 384, 512, 640]
SEEN = [0, 1, 3, 4, 5, 6]
KEYS = NU * P

N_UNIT = HM + HG + 2 * HD


def score_map(h):
    if h < HM:
        return h // 2, h % 2, h // 2, h * 64, 64 ** -0.5
    if h < HM + HG:
        j, g = divmod(h - HM, GKV)
        return 3 + j, g, 3, 384 + g * 64, 64 ** -0.5
    m = h - HM - HG
    return 6 + m // 4, m % 4, 4 + m // 4, 512 + (m // 2) * 64, 32 ** -0.5


def out_column(h):
    if h < HM:
        return h * 64
    if h < HM + HG:
        j, g = divmod(h - HM, GKV)
        return 384 + (g * GJ + j) * 64
    return 768 + ((h - HM - HG) // 2) * 64


MAPS_OF_BLOCK = [[h for h in range(N_UNIT) if score_map(h)[0] == b] for b in range(8)]

WO_COLS = [(0, 384), (384, 768), (768, 1024)]
RING = 4
N_MOD = 12
MOD_MID = 6


def ring_uses():
    uses = [("mod", 0, j) for j in range(N_MOD)]
    for l in range(DEPTH):
        uses += [("in", l, b) for b in range(len(BLK))]
        uses += [("out", l, b) for b in range(len(WO_COLS))]
        if l + 1 < DEPTH:
            uses += [("mod", l + 1, j) for j in range(MOD_MID)]
        uses += [("moe", l, i) for i in range(N_ET)]
        if l + 1 < DEPTH:
            uses += [("mod", l + 1, j) for j in range(MOD_MID, N_MOD)]
    return uses


USES = ring_uses()
USE_AT = {u: g for g, u in enumerate(USES)}
USE_CUM = [16 * sum(u[0] != "moe" for u in USES[g % RING:g + 1:RING]) for g in range(len(USES))]


def trunk(nc, a, o):
    def scratch(name, shape, dt=F32):
        return nc.dram_tensor(name, shape, dt).ap()

    mod_rows = scratch("mod_rows", (DEPTH, 2, 6 * D))
    h_rows = scratch("h_rows", (NT * P, D))
    y_rows = scratch("y_rows", (N_SLOT, D))

    ctx = ExitStack()
    with ctx:
        def sb(name, cols, dt=F32):
            return ctx.enter_context(nc.sbuf_tensor(name, [P, cols], dt))

        def sem(name):
            return ctx.enter_context(nc.semaphore(name))

        x = sb("x", NT * D)
        hT_region = sb("hT_region", KC * NT * P)
        ring = sb("ring", RING * 4096)
        arena = sb("arena", 6 * KEYS + NU * 768 + NT * D)
        qz = sb("qz", 12 * P)
        work = sb("work", 3072)
        k_tok = sb("k_tok", 2 * 640)
        ckvT = sb("ckvT", P)
        ident = sb("ident", P)
        ones = sb("ones", P)
        tri = sb("tri", P)
        rope = sb("rope", NT * 96)
        kv_g = sb("kv_g", RANK)
        qn_g = sb("qn_g", 64)
        kn_g = sb("kn_g", 64)
        df_g = sb("df_g", 64)
        lam_in = sb("lam_in", 128)
        lconst = sb("lconst", 8)
        n1col = sb("n1col", KC)
        w_rt = sb("w_rt", KC * 20)
        b_rt = sb("b_rt", 20)
        wuk = sb("wuk", 3 * P)
        wuv = sb("wuv", 384)
        cond = sb("cond", KC * 2)
        cond_e = sb("cond_e", KC * 2)
        silu_c = sb("silu_c", KC * 2)
        modrow = sb("modrow", 2 * 512)
        modcol = sb("modcol", 2 * 2 * KC)
        small = sb("small", 160)
        negh = sb("negh", 16)
        desc = sb("desc", 4)
        k128 = sb("k128", NT)
        le = sb("le", NE * NE)
        lt = sb("lt", NT * NT)
        iota_t = sb("iota_t", N_ET)
        rout_w = sb("rout_w", 2 * NT)
        tok_id = sb("tok_id", NT)
        lane = sb("lane", P)
        slots_i = sb("slots_i", 2 * NT, I32)
        idx = sb("idx", N_ET, I32)
        experts_i = sb("experts_i", N_ET + 1, I32)
        ps = ctx.enter_context(nc.psum_tensor("ps", [P, 8, 512], F32))

        x_t = [x[:, t * D:(t + 1) * D] for t in range(NT)]
        hT = hT_region[:].rearrange("p (c n) -> p c n", c=KC)
        slot = [ring[:, s * 4096:(s + 1) * 4096] for s in range(RING)]
        kT = arena[:, 0:6 * KEYS].rearrange("p (j n) -> p j n", j=6)
        V0 = 6 * KEYS
        V = arena[:, V0:V0 + NU * 768].rearrange("p (u n) -> p u n", u=NU)
        Q0 = V0 + NU * 768
        q_tok = [arena[:, Q0 + t * D:Q0 + (t + 1) * D] for t in range(NT)]
        gate1c, gate1l = modrow[:], arena[:, 0:1024]
        a2b = arena[:, 2048:4096].rearrange("p (k n) -> p k n", k=2)
        b2b = arena[:, 4096:6144].rearrange("p (k n) -> p k n", k=2)
        gate2b = arena[:, 6144:8192].rearrange("p (k n) -> p k n", k=2)
        gain_b = arena[:, 8192:9216]
        w_dn = [arena[:, 9216 + 2048 * s:9216 + 2048 * (s + 1)] for s in range(2)]
        y_out = [arena[:, 13312 + 1024 * s:13312 + 1024 * (s + 1)] for s in range(2)]
        hg = [hT_region[:, 1024 * s:1024 * (s + 1)] for s in range(2)]
        hgT = [hT_region[:, 2048 + 1024 * s:2048 + 1024 * (s + 1)].rearrange("p (c n) -> p c n", c=KC)
               for s in range(2)]
        y_in = [[v[:, 1024 * k:1024 * (k + 1)] for k in range(2)]
                for v in (hT_region[:, 0:2048], hT_region[:, 2048:4096], w_dn[0], w_dn[1],
                          arena[:, 13312:15360])]
        xn = [work[:, 1024 * s:1024 * (s + 1)] for s in range(2)]
        rope_c = work[:, 2048:2560]
        rope_s = work[:, 2560:3072]
        pr = [work[:, 768 * s:768 * (s + 1)] for s in range(2)]
        prT = [work[:, 1536 + 768 * s:1536 + 768 * (s + 1)] for s in range(2)]
        h2T = work[:, 0:1024].rearrange("p (c n) -> p c n", c=KC)
        h2 = work[:, 1024:2048]
        xo_tmp = work[:, 2048:2432]
        logits = work[:, 2944:3044].rearrange("p (t n) -> p t n", t=NT)
        sig = [work[:, 256 * s:256 * (s + 1)] for s in range(2)]
        hid = [work[:, 512 + 256 * s:512 + 256 * (s + 1)] for s in range(2)]
        hidT = [work[:, 1024 + 256 * s:1024 + 256 * (s + 1)].rearrange("p (c n) -> p c n", c=2)
                for s in range(2)]
        pair_q = [[qz[:, (2 * s + i) * P:(2 * s + i + 1) * P] for i in range(2)] for s in range(2)]
        quad_q = [[qz[:, (4 + 4 * s + i) * P:(5 + 4 * s + i) * P] for i in range(4)] for s in range(2)]
        ss1, rs1 = small[:, 0:5], small[:, 5:10]
        ss9, rs9 = small[:, 10:19], small[:, 20:29]
        inv9 = small[:, 30:39]
        mx = small[:, 40:42]
        negm = small[:, 42:44]
        sums = small[:, 44:84]
        rec = small[:, 84:86]
        lam4 = small[:, 86:90]
        lam = small[:, 90:91]
        ss4, rs4 = small[:, 92:96], small[:, 96:100]
        ss2, rs2 = small[:, 104:109], small[:, 109:114]
        ssf, rsf = small[:, 114:119], small[:, 119:124]
        k_view = [k_tok[:, 640 * s:640 * (s + 1)] for s in range(2)]
        def mod_row(j):
            q, k = divmod(j % 8, 2)
            return modrow[32 * q:32 * q + 2, k * 512:(k + 1) * 512]
        mod_c = modcol[:].rearrange("p (j k c) -> p j k c", j=2, k=2)
        silu_v = silu_c[:].rearrange("p (k c) -> p k c", k=2)

        w_landed = [sem(f"w_landed{s}") for s in range(RING)]
        wgu_landed = [[sem(f"wgu_landed{l}_{s}") for s in range(RING)] for l in range(DEPTH)]
        wd_landed = [[sem(f"wd_landed{l}_{s}") for s in range(2)] for l in range(DEPTH)]
        s_setup_dma = sem("s_setup_dma")
        s_small = sem("s_small")
        s_vcache = sem("s_vcache")
        s_cond = sem("s_cond")
        s_modbias = sem("s_modbias")
        s_rowout = [sem(f"s_rowout{s}") for s in range(3)]
        s_modcol = sem("s_modcol")
        s_ctxout = sem("s_ctxout")
        s_gate1 = sem("s_gate1")
        s_bcast = sem("s_bcast")
        s_hout = sem("s_hout")
        s_hg = [[sem(f"s_hg{l}_{s}") for s in range(2)] for l in range(DEPTH)]
        s_yout = [[sem(f"s_yout{l}_{s}") for s in range(2)] for l in range(DEPTH)]
        s_yin = [sem(f"s_yin{t}") for t in range(NT)]
        s_fill = sem("s_fill")
        s_final = sem("s_final")
        c_const = sem("c_const")
        c_cond = sem("c_cond")
        c_e = sem("c_e")
        x_ready = sem("x_ready")
        mod_done = sem("mod_done")
        mod_evac = sem("mod_evac")
        a1_ready = sem("a1_ready")
        ss1_ready = sem("ss1_ready")
        rs1_ready = sem("rs1_ready")
        xn_ready = sem("xn_ready")
        hT_done = sem("hT_done")
        hT_evac = sem("hT_evac")
        z_done = sem("z_done")
        z_used_d = sem("z_used_d")
        z_used_a = sem("z_used_a")
        ss9_ready = sem("ss9_ready")
        rs9_ready = sem("rs9_ready")
        k_ready = sem("k_ready")
        k1_done = sem("k1_done")
        k2_done = sem("k2_done")
        kA_evac = sem("kA_evac")
        kB_evac = sem("kB_evac")
        qt_done = sem("qt_done")
        qz_d = sem("qz_d")
        qz_a = sem("qz_a")
        s_done = sem("s_done")
        m_ready = sem("m_ready")
        exp_done = sem("exp_done")
        pt4_done = sem("pt4_done")
        pt5_done = sem("pt5_done")
        pt4_evac = sem("pt4_evac")
        pt5_evac = sem("pt5_evac")
        pv_done = sem("pv_done")
        o_evac = sem("o_evac")
        lam_s = sem("lam_s")
        lam_e = sem("lam_e")
        ss4_ready = sem("ss4_ready")
        rs4_ready = sem("rs4_ready")
        o_ready = sem("o_ready")
        oT_done = sem("oT_done")
        oT_evac_d = sem("oT_evac_d")
        oT_evac_a = sem("oT_evac_a")
        wo_done = sem("wo_done")
        xo_done = sem("xo_done")
        ss2_ready = sem("ss2_ready")
        rs2_ready = sem("rs2_ready")
        h2_ready = sem("h2_ready")
        h2T_done = sem("h2T_done")
        h2T_evac_d = sem("h2T_evac_d")
        h2T_evac_a = sem("h2T_evac_a")
        rt_done = sem("rt_done")
        lg_ready = sem("lg_ready")
        r_sub = sem("r_sub")
        r_exp = sem("r_exp")
        r_mask = sem("r_mask")
        r_count = sem("r_count")
        slots_ready = sem("slots_ready")
        r_hot = sem("r_hot")
        r_rows = sem("r_rows")
        idx_ready = sem("idx_ready")
        experts_ready = sem("experts_ready")
        gt_done = [sem(f"gt_done{l}") for l in range(DEPTH)]
        gt_evac_d = [sem(f"gt_evac_d{l}") for l in range(DEPTH)]
        gt_evac_a = [sem(f"gt_evac_a{l}") for l in range(DEPTH)]
        gu_done = [sem(f"gu_done{l}") for l in range(DEPTH)]
        sig_done = [sem(f"sig_done{l}") for l in range(DEPTH)]
        hid_ready = [sem(f"hid_ready{l}") for l in range(DEPTH)]
        ht_done = [sem(f"ht_done{l}") for l in range(DEPTH)]
        ht_evac = [sem(f"ht_evac{l}") for l in range(DEPTH)]
        dn_done = [sem(f"dn_done{l}") for l in range(DEPTH)]
        y_evac_d = [sem(f"y_evac_d{l}") for l in range(DEPTH)]
        y_evac_a = [sem(f"y_evac_a{l}") for l in range(DEPTH)]
        y1_ready = sem("y1_ready")
        eps_in = sem("eps_in")
        f_ss = sem("f_ss")
        f_rs = sem("f_rs")
        f_out = sem("f_out")

        N_Q = NT * 8
        N_S = NT * N_UNIT
        N_S5 = (NT - 1) * N_UNIT

        block = ctx.enter_context(nc.Block())

        def row_b(v, n, parts=P):
            return v.unsqueeze(0).to_broadcast([parts, n])

        def key_norm_rows(pool, l, t, rsqrt):
            pool.wait_ge(ss9_ready, l * NT + t + 1)
            rsqrt(rs9, ss9, 9).then_inc(rs9_ready, 1)
            if t == 0:
                pool.wait_ge(k_ready, l * NT + 1)
                pool.wait_ge(z_used_a, l * 3 * NT + 3)
                kb = k_view[0]
                for dst, src in (
                        (o["new_mla_ckv"][0, l], kb[:, 0:128]),
                        (o["new_mla_krope"][0, l], kb[:, 160:192]),
                        (o["new_gqa_k"][0, l].rearrange("s g n -> s (g n)"), kb[:, 256:384]),
                        (o["new_diff_k"][0, l].rearrange("s h k n -> s (h k n)"), kb[:, 384:640]),
                        (o["new_gqa_v"][0, l].rearrange("s g n -> s (g n)"), V[:, 2, 384:512]),
                        (o["new_diff_v"][0, l].rearrange("s h n -> s (h n)"), V[:, 2, 512:768])):
                    pool.dma_start(dst, src).then_inc(s_ctxout, 16)

        def y_copy_a(act, l, i):
            with if_used(act, i):
                act.wait_ge(dn_done[l], i + 1)
                y_buffer_free(act, l, i)
                act.activation(y_out[i % 2][:, 512:1024], ps[:, 6, :], ACT.Copy).then_inc(y_evac_a[l], 1)

        def y_buffer_free(eng, l, i):
            if i >= 2:
                eng.wait_ge(s_yout[l][i % 2], 16 * (i // 2))

        tiles_used = {}

        def load_tiles_used(eng, l):
            eng.wait_ge(experts_ready, l + 1)
            tiles_used[eng] = eng.value_load(experts_i[0:1, N_ET:N_ET + 1], min_val=MIN_ET, max_val=N_ET)

        def if_used(eng, i):
            return eng.If(tiles_used[eng] > i) if i >= MIN_ET else nullcontext()

        RT = [0]

        def rt(n, base=work):
            v = base[:, RT[0]:RT[0] + n]
            RT[0] += n
            return v

        def v3(v, n):
            return v.rearrange("p (t n) -> p t n", n=n)

        def v4(v):
            return v.rearrange("p (t g e) -> p t g e", t=NT, g=NGRP)
        r_gm, r_gs, r_gex, r_gtop = rt(5), rt(20), rt(20), rt(5)
        r_t1, r_t2, r_t3, r_og = rt(20), rt(20), rt(5), rt(20)
        r_sel, r_es, r_m1, r_m2, r_o1, r_o2 = rt(80), rt(20), rt(5), rt(5), rt(20), rt(20)
        r_es2, r_d, r_ex2, r_den = rt(20), rt(5), rt(5), rt(5)
        r_O1, r_O2, r_M = rt(80), rt(80), rt(80)
        r_cn, r_rank, r_big, r_add = rt(80), rt(80), rt(400), rt(80)
        r_c, r_nt, r_incl, r_excl = rt(16), rt(16), rt(16), rt(16)
        r_sl, r_tl, r_ex = rt(2 * NT), rt(2 * NT), rt(N_ET)
        assert RT[0] <= 2048
        tile_hot = hT_region[:, 2048:2048 + 2 * NT * N_ET].rearrange("p (k i) -> p k i", i=N_ET)
        pair_tok = hT_region[:, 2560:2560 + 2 * NT * N_ET].rearrange("p (k i) -> p k i", i=N_ET)
        place_hot = hT_region[:, 3072:3072 + 2 * NT * P].rearrange("p (k n) -> p k n", n=P)

        @block.sync
        def _(sp):
            for k, src in enumerate((a["c_ctx"], a["c"][0])):
                sp.dma_start(cond[:, k * KC:(k + 1) * KC], src.rearrange("(p c) -> p c", c=KC)).then_inc(s_cond, 16)

            def slot_free(g):
                uk, ul, ui = USES[g - RING]
                if uk == "mod":
                    sp.wait_ge(mod_done, ul * N_MOD + ui + 1)
                elif uk == "in":
                    sp.wait_ge(z_done, ul * 4 * NT + 4 * (NT - 1) + ui + 1)
                elif uk == "out":
                    sp.wait_ge(wo_done, ul * 15 + 3 * (NT - 1) + ui + 1)
                elif USES[g][0] == "moe":
                    sp.wait_ge(gu_done[ul], ui + 1)
                else:
                    for tile in range(ui % RING, ui + 1, RING):
                        if tile >= MIN_ET - RING:
                            with if_used(sp, tile):
                                sp.wait_ge(gu_done[ul], tile + 1)

            def tile_expert(l, i):
                return sp.snap(l * NE + sp.value_load(experts_i[0:1, i:i + 1], min_val=0, max_val=NE - 1))

            def down_weights(l, i):
                with if_used(sp, i):
                    if i >= 2:
                        sp.wait_ge(dn_done[l], i - 1)
                    else:
                        sp.wait_ge(wo_done, l * 15 + 15)
                    sp.dma_start(w_dn[i % 2].rearrange("p (c n) -> p c n", c=2),
                                 a["moe_w_down"].rearrange("l e (p c) n -> (l e) p c n", c=2)[tile_expert(l, i)]
                                 ).then_inc(wd_landed[l][i % 2], 16)

            for g, (kind, l, i) in enumerate(USES):
                if kind == "moe" and i == 0:
                    load_tiles_used(sp, l)
                if kind == "moe" and i == 1:
                    sp.wait_ge(s_hg[l][0], 16)
                to = slot[g % RING]
                if kind == "moe":
                    with if_used(sp, i):
                        slot_free(g)
                        dst = to.rearrange("p (c k n) -> p c k n", c=KC, k=2)
                        e = tile_expert(l, i)
                        for k, name in enumerate(("moe_w_gate", "moe_w_up")):
                            sp.dma_start(dst[:, :, k, :],
                                         a[name].rearrange("l e (p c) f -> (l e) p c f", c=KC)[e]
                                         ).then_inc(wgu_landed[l][i % RING], 16)
                    if i >= 1:
                        down_weights(l, i - 1)
                    if i == N_ET - 1:
                        down_weights(l, i)
                    continue
                if kind == "mod" and l >= 1 and i == MOD_MID + 3:
                    sp.wait_ge(s_yin[1], l * 32)
                if g >= RING:
                    slot_free(g)
                name, (c0, c1) = {"mod": ("w_mod", (i * 512, (i + 1) * 512)), "in": ("w_in", BLK[min(i, 3)]),
                                  "out": ("w_out", WO_COLS[min(i, 2)])}[kind]
                sp.dma_start(to[:, 0:KC * (c1 - c0)].rearrange("p (c n) -> p c n", c=KC),
                             a[name][l].rearrange("(p c) n -> p c n", c=KC)[:, :, c0:c1]
                             ).then_inc(w_landed[g % RING], 16)

        @block.gpsimd
        def _(pool):
            dma = pool.dma_start
            for v in (ident[:], wuk[:], qz[:], k_tok[:]):
                pool.memset(v, 0.0)
            pool.memset(tri[:], 1.0)
            pool.memset(ones[:], 1.0)
            pool.memset(le[:], 1.0)
            pool.memset(lt[:], 1.0)
            pool.memset(negh[:], -0.5)
            pool.memset(inv9[:, 0:1], 1.0 / RANK)
            pool.memset(inv9[:, 1:9], 1.0 / 64)
            pool.iota(desc[:], pattern=[[-1, 4]], base=4, channel_multiplier=0,
                      allow_small_or_imprecise_dtypes=True)
            pool.iota(k128[:], pattern=[[P, NT]], base=0, channel_multiplier=0,
                      allow_small_or_imprecise_dtypes=True)
            pool.iota(iota_t[:], pattern=[[1, N_ET]], base=0, channel_multiplier=0,
                      allow_small_or_imprecise_dtypes=True)
            pool.iota(tok_id[:], pattern=[[P, NT]], base=0, channel_multiplier=1,
                      allow_small_or_imprecise_dtypes=True)
            pool.iota(lane[:], pattern=[[1, P]], base=0, channel_multiplier=0,
                      allow_small_or_imprecise_dtypes=True)
            pool.drain()
            pool.affine_select(out=ident[:], in_=ident[:], compare_op=ALU.not_equal, fill=1.0, base=0,
                               pattern=[[-1, P]], channel_multiplier=1)
            pool.affine_select(out=tri[:], in_=tri[:], compare_op=ALU.is_gt, fill=0.0, base=0,
                               pattern=[[1, P]], channel_multiplier=-1)
            pool.affine_select(out=lt[:], in_=lt[:], compare_op=ALU.is_gt, fill=0.0, base=0,
                               pattern=[[1, NT], [-1, NT]], channel_multiplier=0)
            pool.affine_select(out=le[:], in_=le[:], compare_op=ALU.is_ge, fill=0.0, base=0,
                               pattern=[[1, NE], [-1, NE]], channel_multiplier=0)
            pool.drain()
            pool.sem_inc(c_const, 1)
            dma(x_t[0], a["x_prompt"][0]).then_inc(s_setup_dma, 16)
            dma(x[:, D:].rearrange("p (t n) -> p t n", t=NT - 1),
                a["x_sample"][0].rearrange("(t p) n -> p t n", p=P)).then_inc(s_setup_dma, 16)
            for l in range(DEPTH):
                for k in range(2):
                    dma(mod_rows[l, k], a["b_mod"][l]).then_inc(s_modbias, 16)
            dma(rope[:].rearrange("p (t n) -> p t n", t=NT),
                a["rope_table"].rearrange("(t p) n -> p t n", p=P)).then_inc(s_setup_dma, 16)

            roots = [0]

            def rsqrt(out, v, n):
                pool.tensor_scalar(v, v, EPS, None, ALU.add).then_inc(eps_in, 1)
                roots[0] += 1
                pool.wait_ge(eps_in, roots[0])
                return pool.tensor_tensor(out, v, negh[:, 0:n], ALU.pow)

            def mod_store(l, j):
                pool.wait_ge(mod_evac, l * N_MOD + j + 1)
                dma(mod_rows[l, :, j * 512:(j + 1) * 512], mod_row(j), accum_op=ALU.add
                    ).then_inc(s_rowout[j // 4], 16)

            def mod_columns(l):
                pool.wait_ge(s_rowout[0], 64 * (l + 1))
                if l >= 1:
                    pool.wait_ge(hT_evac, l * 2 * NT + 1)
                for k in range(2):
                    dma(mod_c[:, :, k, :],
                        mod_rows[l, k, 0:2 * D].rearrange("(j p c) -> p j c", j=2, c=KC)
                        ).then_inc(s_modcol, 16)

            def small_in(l):
                return [
                    (kv_g[:], row_b(a["mla_kv_norm_g"][l], RANK)),
                    (qn_g[:], row_b(a["gqa_q_norm_g"][l], 64)),
                    (kn_g[:], row_b(a["gqa_k_norm_g"][l], 64)),
                    (df_g[:], row_b(a["diff_norm_g"][l], 64)),
                    (lam_in[:], row_b(a["diff_lambda"].rearrange("l a b -> l (a b)")[l], 128)),
                    (lconst[:], row_b(a["layer_consts"][l], 8)),
                    (n1col[:], a["norm1_g"].rearrange("l (p c) -> l p c", c=KC)[l]),
                    (w_rt[:].rearrange("p (c n) -> p c n", c=KC)[:, :, 0:4],
                     a["moe_w_group"].rearrange("l (p c) n -> l p c n", c=KC)[l]),
                    (w_rt[:].rearrange("p (c n) -> p c n", c=KC)[:, :, 4:20],
                     a["moe_w_router"].rearrange("l (p c) n -> l p c n", c=KC)[l]),
                    (b_rt[:, 0:4], row_b(a["moe_b_group"][l], 4)),
                    (b_rt[:, 4:20], row_b(a["moe_b_router"][l], 16)),
                    (wuk[:].rearrange("p (h n) -> p h n", h=HM)[:, :, 0:32], a["mla_w_uk"][l]),
                    (wuv[:], a["mla_w_uv"].rearrange("l r h e -> l r (h e)")[l]),
                    (k_tok[:].rearrange("p (b n) -> p b n", b=2)[:, :, 0:128],
                     a["cache_mla_ckv"][0, l].rearrange("(b p) n -> p b n", p=P)),
                    (k_tok[:].rearrange("p (b n) -> p b n", b=2)[:, :, 160:192],
                     a["cache_mla_krope"][0, l].rearrange("(b p) n -> p b n", p=P)),
                    (k_tok[:].rearrange("p (b n) -> p b n", b=2)[:, :, 224:256],
                     a["cache_mla_krope"][0, l].rearrange("(b p) n -> p b n", p=P)),
                    (k_tok[:].rearrange("p (b n) -> p b n", b=2)[:, :, 256:384],
                     a["cache_gqa_k"][0, l].rearrange("(b p) g n -> p b (g n)", p=P)),
                    (k_tok[:].rearrange("p (b n) -> p b n", b=2)[:, :, 384:640],
                     a["cache_diff_k"][0, l].rearrange("(b p) h k n -> p b (h k n)", p=P)),
                ]

            def small_loads(l, k0, k1):
                for dst, src in small_in(l)[k0:k1]:
                    dma(dst, src).then_inc(s_small, 16)

            def value_loads(l):
                pool.wait_ge(x_ready, l * NT + NT)
                dma(V[:, 0:2, 384:512], a["cache_gqa_v"][0, l].rearrange("(b p) g n -> p b (g n)", p=P)
                    ).then_inc(s_vcache, 16)
                dma(V[:, 0:2, 512:768], a["cache_diff_v"][0, l].rearrange("(b p) h n -> p b (h n)", p=P)
                    ).then_inc(s_vcache, 16)

            def norm1_root(l, t):
                pool.wait_ge(ss1_ready, l * NT + t + 1)
                rsqrt(rs1[:, t:t + 1], ss1[:, t:t + 1], 1).then_inc(rs1_ready, 1)

            small_loads(0, 0, N_SMALL_IN)
            value_loads(0)
            pool.wait_ge(s_modbias, 64)
            for l in range(DEPTH):
                if l == 0:
                    for j in range(N_MOD):
                        mod_store(0, j)
                        if j == 3:
                            mod_columns(0)
                        if j >= N_MOD - 3 and j < N_MOD - 1:
                            norm1_root(0, j - (N_MOD - 3))

                for t in range(NT):
                    if t >= 2:
                        norm1_root(l, t)
                    if t >= 1:
                        key_norm_rows(pool, l, t - 1, rsqrt)
                key_norm_rows(pool, l, NT - 1, rsqrt)

                if l == 0:
                    dma(y_rows[MIN_ET * P:, :].rearrange("(i p) n -> p i n", p=P),
                        x_t[0].unsqueeze(1).to_broadcast([P, N_ET - MIN_ET, D])).then_inc(s_fill, 16)

                for t in range(NT):
                    pool.wait_ge(ss4_ready, l * NT + t + 1)
                    rsqrt(rs4, ss4, 4).then_inc(rs4_ready, 1)

                for k in range(3):
                    pool.wait_ge(s_rowout[k], 64 * (l + 1))
                dma(gate1c, row_b(mod_rows[l, 0, 2 * D:3 * D], D)).then_inc(s_gate1, 16)
                pool.wait_ge(pv_done, l * N_S + N_S)
                pool.wait_ge(s_ctxout, l * 96 + 96)
                dma(gate1l, row_b(mod_rows[l, 1, 2 * D:3 * D], D)).then_inc(s_gate1, 16)

                def rows(dst, j):
                    for k in range(2):
                        dma(dst[:, k, :], row_b(mod_rows[l, k, j * D:(j + 1) * D], D)
                            ).then_inc(s_bcast, 16)
                rows(a2b, 4)
                rows(b2b, 3)
                rows(gate2b, 5)
                dma(gain_b, row_b(a["norm2_g"][l], D)).then_inc(s_bcast, 16)

                for t in range(NT):
                    pool.wait_ge(ss2_ready, l * NT + t + 1)
                    rsqrt(rs2[:, t:t + 1], ss2[:, t:t + 1], 1).then_inc(rs2_ready, 1)
                    pool.wait_ge(h2_ready, l * NT + t + 1)
                    dma(h_rows[t * P:(t + 1) * P, :], h2).then_inc(s_hout, 16)

                if l + 1 < DEPTH:
                    mod_store(l + 1, 0)
                pool.wait_ge(slots_ready, l + 1)
                pool.wait_ge(idx_ready, l + 1)
                pool.wait_ge(s_hout, l * 80 + 80)

                if l == 0:
                    pool.wait_ge(s_fill, 16)

                def y_store(i):
                    with if_used(pool, i):
                        pool.wait_ge(y_evac_d[l], i + 1)
                        pool.wait_ge(y_evac_a[l], i + 1)
                        dma(y_rows[i * P:(i + 1) * P, :], y_out[i % 2]).then_inc(s_yout[l][i % 2], 16)

                load_tiles_used(pool, l)

                for i in range(N_ET):
                    with if_used(pool, i):
                        if i < 2:
                            pool.wait_ge(wo_done, l * 15 + 15)
                        else:
                            pool.wait_ge(gt_done[l], i - 1)
                        pool.indirect_dma_start(
                            out=hg[i % 2], out_offset=None, in_=h_rows,
                            in_offset=bass.IndirectOffsetOnAxis(ap=idx[:, i:i + 1], axis=0)
                        ).then_inc(s_hg[l][i % 2], 16)
                    if i >= 3:
                        y_store(i - 3)
                    if i == 1 and l + 1 < DEPTH:
                        for j in range(1, MOD_MID):
                            mod_store(l + 1, j)
                        mod_columns(l + 1)
                    if 3 <= i < 9 and l + 1 < DEPTH:
                        small_loads(l + 1, 3 * (i - 3), 3 * (i - 2))
                for i in range(N_ET - 3, N_ET):
                    y_store(i)
                for i in range(MIN_ET - 2, N_ET):
                    with if_used(pool, i):
                        pool.wait_ge(s_yout[l][i % 2], 16 * (i // 2 + 1))
                for t in range(NT):
                    for k in range(2):
                        pool.indirect_dma_start(
                            out=y_in[t][k], out_offset=None, in_=y_rows,
                            in_offset=bass.IndirectOffsetOnAxis(ap=slots_i[:, k * NT + t:k * NT + t + 1], axis=0)
                        ).then_inc(s_yin[t], 16)
                if l + 1 < DEPTH:
                    norm1_root(l + 1, 0)
                    for j in range(MOD_MID, N_MOD - 2):
                        mod_store(l + 1, j)
                    norm1_root(l + 1, 1)
                    value_loads(l + 1)
                    for j in range(N_MOD - 2, N_MOD):
                        mod_store(l + 1, j)

            def y_leaves(t):
                pool.wait_ge(f_out, t + 1)
                dst = o["y_prompt"][0] if t == 0 else o["y_sample"][0, (t - 1) * P:t * P, :]
                dma(dst, x_t[t]).then_inc(s_final, 16)

            dma(gain_b, row_b(a["final_norm_g"], D)).then_inc(s_final, 16)
            for t in range(NT):
                pool.wait_ge(f_ss, t + 1)
                rsqrt(rsf[:, t:t + 1], ssf[:, t:t + 1], 1).then_inc(f_rs, 1)
                if t >= 1:
                    y_leaves(t - 1)
            y_leaves(NT - 1)
            pool.wait_ge(s_final, 16 * (NT + 1))
            pool.wait_ge(s_ctxout, DEPTH * 96)

        @block.scalar
        def _(act):
            act.wait_ge(s_cond, 32)
            act.activation(cond_e[:], cond[:], ACT.Exp, scale=-1.0).then_inc(c_e, 1)

            def mod_copy(l, j):
                act.wait_ge(mod_done, l * N_MOD + j + 1)
                if j >= 8:
                    act.wait_ge(s_rowout[0], 64 * (l + 1))
                elif l >= 1:
                    act.wait_ge(s_rowout[j // 4], 64 * l)
                    act.wait_ge(s_rowout[2], 64 * l)
                act.activation(mod_row(j), ps[0:2, 2 + j % 2, :], ACT.Copy).then_inc(mod_evac, 1)

            def norm1_sums(l, t):
                act.wait_ge(x_ready, l * NT + t + 1)
                if t >= 2:
                    act.wait_ge(hT_done, l * 2 * NT + 2 * (t - 1))
                act.activation(xn[t % 2], x_t[t], ACT.Square, scale=D ** -0.5,
                               accum_out=ss1[:, t:t + 1]).then_inc(ss1_ready, 1)

            for j in range(N_MOD):
                mod_copy(0, j)
                if j in (3, 4):
                    norm1_sums(0, j - 3)

            def final_sums(t):
                act.wait_ge(x_ready, DEPTH * NT + t + 1)
                act.activation(work[:, 1024 * (t % 2):1024 * (t % 2 + 1)], x_t[t], ACT.Square, scale=D ** -0.5,
                               accum_out=ssf[:, t:t + 1]).then_inc(f_ss, 1)
                act.drain()

            for l in range(DEPTH):
                def hT_copy(t):
                    act.wait_ge(hT_done, l * 2 * NT + 2 * t + 2)
                    act.wait_ge(a1_ready, l + 1)
                    for q in range(4):
                        c = 4 + q
                        k = min(t, 1)
                        last = act.activation(hT[:, c, t * P:(t + 1) * P], ps[:, 7, q * P:(q + 1) * P],
                                              ACT.Identity, bias=mod_c[:, 0, k, c:c + 1],
                                              scale=mod_c[:, 1, k, c:c + 1])
                    last.then_inc(hT_evac, 1)

                def z_copies(t):
                    act.wait_ge(z_used_d, l * 4 * NT + 4 * t + 1)
                    act.activation(q_tok[t][:, 0:384].rearrange("p (h n) -> p h n", h=HM)[:, :, 0:32],
                                   ps[:, 0, 0:384].rearrange("p (h n) -> p h n", h=HM)[:, :, 0:32],
                                   ACT.Copy).then_inc(z_used_a, 1)
                    act.wait_ge(z_used_d, l * 4 * NT + 4 * t + 3)
                    act.activation(V[:, 2 + t, 384:512], ps[:, 2, 128:256], ACT.Copy).then_inc(z_used_a, 1)
                    act.wait_ge(z_used_d, l * 4 * NT + 4 * t + 4)
                    act.activation(V[:, 2 + t, 512:768], ps[:, 3, 256:512], ACT.Copy).then_inc(z_used_a, 1)

                def key_copies_a(u):
                    act.wait_ge(k1_done, l * NU + u + 1)
                    act.wait_ge(k2_done, l * NU + u + 1)
                    act.activation(ckvT[:], ps[:, 4, 0:128], ACT.Copy)
                    act.activation(kT[:, 3:6, KCOL[u]:KCOL[u] + P],
                                   ps[:, 4, 128:512].rearrange("p (j n) -> p j n", j=3),
                                   ACT.Copy).then_inc(kA_evac, 1)

                def key_copies_b(u):
                    act.wait_ge(k2_done, l * NU + u + 2)
                    act.activation(kT[:, 0:3, KCOL[u]:KCOL[u] + P],
                                   ps[:, 5, 0:384].rearrange("p (j n) -> p j n", j=3), ACT.Copy)
                    act.activation(V[:, u, 0:384], ps[:, 6, 0:384], ACT.Copy).then_inc(kB_evac, 1)

                hT_copy(0)
                act.wait_ge(x_ready, l * NT + NT)
                for u in range(2):
                    key_copies_a(u)
                    key_copies_b(u)
                for t in range(NT):
                    if t >= 1:
                        key_copies_a(1 + t)
                    if t + 2 < NT:
                        norm1_sums(l, t + 2)
                    z_copies(t)
                    if t >= 1:
                        key_copies_b(1 + t)
                    if t + 1 < NT:
                        hT_copy(t + 1)
                key_copies_a(NU - 1)
                key_copies_b(NU - 1)

                act.wait_ge(lam_s, l + 1)
                act.activation(lam4[:, 2:4], lam4[:, 0:2], ACT.Exp).then_inc(lam_e, 1)

                def query_copies(gb):
                    b = gb % 8
                    act.wait_ge(qt_done, l * N_Q + gb + 1)
                    src = ps[:, 7, (gb % 2) * P:(gb % 2 + 1) * P]
                    if b < 6:
                        act.activation(pair_q[b % 2][1][64:128, :], src[64:128, :], ACT.Copy).then_inc(qz_a, 1)
                    else:
                        act.activation(quad_q[b % 2][2][64:96, :], src[64:96, :], ACT.Copy)
                        act.activation(quad_q[b % 2][3][96:128, :], src[96:128, :], ACT.Copy).then_inc(qz_a, 1)

                def probs(n):
                    t, h = divmod(n, N_UNIT)
                    act.wait_ge(m_ready, l * N_S + n + 1)
                    if n >= 2:
                        act.wait_ge(pt4_done, l * N_S + n - 1)
                        if n - 2 >= N_UNIT:
                            act.wait_ge(pt5_done, l * N_S5 + n - 1 - N_UNIT)
                    b0 = 2 * (n % 2)
                    col = sums[:, h + N_UNIT * (t % 2):h + N_UNIT * (t % 2) + 1]
                    if t == 0:
                        i_, o_ = ps[:, b0, 0:P], pr[n % 2][:, 0:P]
                    else:
                        i_ = ps[:, b0:b0 + 2, 0:384]
                        o_ = pr[n % 2].rearrange("p (a n) -> p a n", a=2)
                    act.activation(o_, i_, ACT.Exp, bias=negm[:, n % 2:n % 2 + 1], scale=score_map(h)[4],
                                   accum_out=col).then_inc(exp_done, 1)

                def probsT(n):
                    if n < N_UNIT:
                        act.wait_ge(pt4_done, l * N_S + n + 1)
                        if n >= 2:
                            act.wait_ge(pv_done, l * N_S + n - 1)
                        act.activation(prT[n % 2][:, 0:P], ps[:, 4, 0:P], ACT.Copy).then_inc(pt4_evac, 1)
                        return
                    act.wait_ge(pt5_done, l * N_S5 + n - N_UNIT + 1)
                    act.wait_ge(pv_done, l * N_S + n - 1)
                    act.activation(prT[n % 2][:, 384:768], ps[:, 5, 0:384], ACT.Copy).then_inc(pt5_evac, 1)

                for n in range(N_S + 1):
                    if n < N_S:
                        h = n % N_UNIT
                        b = score_map(h)[0]
                        if h == MAPS_OF_BLOCK[b][0]:
                            gb = 8 * (n // N_UNIT) + b
                            if gb == 0:
                                query_copies(0)
                            if gb + 1 < N_Q:
                                query_copies(gb + 1)
                    if n >= 1:
                        probsT(n - 1)
                    if n < N_S:
                        probs(n)

                def oT_copy(t):
                    act.wait_ge(oT_done, l * 2 * NT + 2 * t + 2)
                    act.activation(hT[:, 4:8, t * P:(t + 1) * P],
                                   ps[:, 5, :].rearrange("p (c n) -> p c n", c=4), ACT.Copy).then_inc(oT_evac_a, 1)

                def norm2_sums(t):
                    act.wait_ge(xo_done, l * 15 + 3 * t + 3)
                    if t >= 1:
                        act.wait_ge(h2T_done, l * 2 * NT + 2 * t)
                        act.wait_ge(s_hout, l * 80 + 16 * t)
                    act.activation(h2, x_t[t], ACT.Square, scale=D ** -0.5,
                                   accum_out=ss2[:, t:t + 1]).then_inc(ss2_ready, 1)

                def h2T_copy(t):
                    act.wait_ge(h2T_done, l * 2 * NT + 2 * t + 2)
                    if t >= 1:
                        act.wait_ge(rt_done, l * NT + t)
                    act.activation(h2T[:, 4:8, :], ps[:, 7, :].rearrange("p (c n) -> p c n", c=4),
                                   ACT.Copy).then_inc(h2T_evac_a, 1)

                oT_copy(0)
                for t in range(NT):
                    if t + 1 < NT:
                        oT_copy(t + 1)
                    norm2_sums(t)
                    h2T_copy(t)

                act.wait_ge(r_sub, 2 * l + 1)
                act.activation(r_gex, r_gs, ACT.Exp).then_inc(r_exp, 1)
                act.wait_ge(r_sub, 2 * l + 2)
                act.activation(r_ex2, r_d, ACT.Exp).then_inc(r_exp, 1)
                if l + 1 < DEPTH:
                    for j in range(MOD_MID):
                        mod_copy(l + 1, j)

                def rows_in(i):
                    with if_used(act, i):
                        act.wait_ge(gt_done[l], i + 1)
                        if i >= 2:
                            act.wait_ge(gu_done[l], i - 1)
                        act.activation(hgT[i % 2][:, 4:8, :], ps[:, 1, :].rearrange("p (c n) -> p c n", c=4),
                                       ACT.Copy).then_inc(gt_evac_a[l], 1)

                def gate_exp(i):
                    with if_used(act, i):
                        act.wait_ge(gu_done[l], i + 1)
                        if i >= 2:
                            act.wait_ge(hid_ready[l], i - 1)
                        act.activation(sig[i % 2], ps[:, 2 + i % 2, 0:FF], ACT.Exp, scale=-1.0
                                       ).then_inc(sig_done[l], 1)

                load_tiles_used(act, l)
                rows_in(0)
                for i in range(N_ET + 1):
                    if i < N_ET:
                        gate_exp(i)
                    if i + 1 < N_ET:
                        rows_in(i + 1)
                    if i >= 1:
                        y_copy_a(act, l, i - 1)

                def scale_first(t):
                    act.wait_ge(s_yin[t], l * 32 + 32)
                    act.activation(y_in[t][0], y_in[t][0], ACT.Copy, scale=rout_w[:, t:t + 1]).then_inc(y1_ready, 1)

                if l + 1 < DEPTH:
                    mod_copy(l + 1, MOD_MID)
                    mod_copy(l + 1, MOD_MID + 1)
                    scale_first(0)
                    scale_first(1)
                    norm1_sums(l + 1, 0)
                    mod_copy(l + 1, MOD_MID + 2)
                    scale_first(2)
                    norm1_sums(l + 1, 1)
                    for t in range(3, NT):
                        scale_first(t)
                    for j in range(MOD_MID + 3, N_MOD):
                        mod_copy(l + 1, j)
                else:
                    scale_first(0)
                    for t in range(NT):
                        if t + 1 < NT:
                            scale_first(t + 1)
                        final_sums(t)

        @block.vector
        def _(dve):
            tt, ts, stt, cp = dve.tensor_tensor, dve.tensor_scalar, dve.scalar_tensor_tensor, dve.tensor_copy
            red = dve.tensor_reduce
            dve.wait_ge(c_e, 1)
            ts(cond_e[:], cond_e[:], 1.0, None, ALU.add)
            dve.drain()
            dve.reciprocal(cond_e[:], cond_e[:])
            dve.drain()
            tt(silu_c[:], cond[:], cond_e[:], ALU.mult).then_inc(c_cond, 1)
            dve.wait_ge(c_const, 1)
            dve.wait_ge(s_setup_dma, 48)
            dve.sem_inc(x_ready, NT)
            dve.sem_inc(o_evac, 1)

            def final_scale(t):
                dve.wait_ge(s_final, 16)
                dve.wait_ge(f_rs, t + 1)
                stt(x_t[t], x_t[t], rsf[:, t:t + 1], gain_b, ALU.mult, ALU.mult).then_inc(f_out, 1)

            for l in range(DEPTH):
                dve.wait_ge(s_modcol, l * 32 + 32)
                dve.wait_ge(s_small, (l + 1) * (16 * N_SMALL_IN))
                for k in range(2):
                    last = stt(mod_c[:, 1, k, :], mod_c[:, 1, k, :], 1.0, n1col[:], ALU.add, ALU.mult)
                last.then_inc(a1_ready, 1)

                def norm_x(t):
                    dve.wait_ge(rs1_ready, l * NT + t + 1)
                    ts(xn[t % 2], x_t[t], rs1[:, t:t + 1], None, ALU.mult).then_inc(xn_ready, 1)

                def hT_copy(t):
                    dve.wait_ge(hT_done, l * 2 * NT + 2 * t + 1)
                    for c in range(4):
                        k = min(t, 1)
                        last = ts(hT[:, c, t * P:(t + 1) * P], ps[:, 7, c * P:(c + 1) * P],
                                  mod_c[:, 1, k, c:c + 1], mod_c[:, 0, k, c:c + 1], ALU.mult, ALU.add)
                    last.then_inc(hT_evac, 1)

                def rotate(t, src, H, w, outs):
                    tab = rope[:, t * 96:(t + 1) * 96]
                    cos, sin = (tab[:, 0:16], tab[:, 16:32]) if w == 16 else (tab[:, 32:64], tab[:, 64:96])
                    n = H * 2 * w
                    C = rope_c[:, 0:n].rearrange("p (h k w) -> p h k w", h=H, k=2)
                    S = rope_s[:, 0:n].rearrange("p (h k w) -> p h k w", h=H, k=2)
                    s4 = src.rearrange("p h (k w) -> p h k w", k=2)
                    tt(C, s4, cos.unsqueeze(1).unsqueeze(1).to_broadcast([P, H, 2, w]), ALU.mult)
                    first = tt(S, s4, sin.unsqueeze(1).unsqueeze(1).to_broadcast([P, H, 2, w]), ALU.mult)
                    dve.drain()
                    for o_ in outs:
                        tt(o_[:, :, 0:w], C[:, :, 0, :], S[:, :, 1, :], ALU.subtract)
                        last = tt(o_[:, :, w:2 * w], S[:, :, 0, :], C[:, :, 1, :], ALU.add)
                    dve.drain()
                    return last

                def z_block(t, b):
                    dve.wait_ge(z_done, l * 4 * NT + 4 * t + b + 1)
                    z = ps[:, b, :]
                    kt = k_view[t % 2]
                    junk = rope_c[:, 0:384]
                    if b == 0:
                        dve.wait_ge(k2_done, l * NU + t + 2)
                        if t == 2:
                            dve.wait_ge(s_ctxout, l * 96 + 96)
                        rotate(t, z[:, 0:384].rearrange("p (h n) -> p h n", h=HM)[:, :, 32:64], HM, 16,
                               [q_tok[t][:, 0:384].rearrange("p (h n) -> p h n", h=HM)[:, :, 32:64]])
                        tt(kt[:, 0:128], z[:, 384:512], kv_g[:], ALU.mult)
                        cp(junk[:, 0:128], z[:, 384:512])
                        dve.drain()
                        tt(junk[:, 0:128], junk[:, 0:128], junk[:, 0:128], ALU.mult).then_inc(z_used_d, 1)
                        dve.drain()
                        red(ss9[:, 0:1], junk[:, 0:128], AX.X, ALU.add)
                        dve.drain()
                    elif b == 1:
                        rotate(t, z[:, 0:32].unsqueeze(1), 1, 16,
                               [kt[:, 160:192].unsqueeze(1), kt[:, 224:256].unsqueeze(1)])
                        qv = z[:, 32:416]
                        cp(junk, qv)
                        qd_ = q_tok[t][:, 384:768]
                        tt(qd_.rearrange("p (j g n) -> p g j n", j=GJ, g=GKV),
                           qv.rearrange("p (g j n) -> p g j n", j=GJ, g=GKV),
                           qn_g[:].unsqueeze(1).unsqueeze(1).to_broadcast([P, GKV, GJ, 64]),
                           ALU.mult).then_inc(z_used_d, 1)
                        dve.drain()
                        tt(junk, junk, junk, ALU.mult)
                        dve.drain()
                        red(ss9[:, 1:7].rearrange("p (j g) -> p g j", j=GJ),
                            junk.rearrange("p (g j n) -> p g j n", j=GJ, g=GKV), AX.X, ALU.add)
                        dve.drain()
                        q3 = qd_.rearrange("p (h n) -> p h n", h=HG)
                        rotate(t, q3, HG, 32, [q3])
                    elif b == 2:
                        kv = z[:, 0:128]
                        cp(junk[:, 0:128], kv)
                        kd_ = kt[:, 256:384]
                        tt(kd_.rearrange("p (g n) -> p g n", g=GKV), kv.rearrange("p (g n) -> p g n", g=GKV),
                           kn_g[:].unsqueeze(1).to_broadcast([P, GKV, 64]), ALU.mult)
                        dve.drain()
                        tt(junk[:, 0:128], junk[:, 0:128], junk[:, 0:128], ALU.mult)
                        dve.drain()
                        red(ss9[:, 7:9], junk[:, 0:128].rearrange("p (g n) -> p g n", g=GKV), AX.X, ALU.add)
                        dve.drain()
                        tt(ss9, ss9, inv9, ALU.mult).then_inc(ss9_ready, 1)
                        k3 = kd_.rearrange("p (g n) -> p g n", g=GKV)
                        rotate(t, k3, GKV, 32, [k3])
                        rotate(t, z[:, 256:512].rearrange("p (h n) -> p h n", h=8), 8, 16,
                               [q_tok[t][:, 768:1024].rearrange("p (h n) -> p h n", h=8)]).then_inc(z_used_d, 1)
                    else:
                        rotate(t, z[:, 0:256].rearrange("p (h n) -> p h n", h=8), 8, 16,
                               [kt[:, 384:640].rearrange("p (h n) -> p h n", h=8)]).then_inc(z_used_d, 1)
                        dve.wait_ge(rs9_ready, l * NT + t + 1)
                        ts(kt[:, 0:128], kt[:, 0:128], rs9[:, 0:1], None, ALU.mult)
                        q3 = q_tok[t][:, 384:768].rearrange("p (h n) -> p h n", h=HG)
                        tt(q3, q3, rs9[:, 1:7].unsqueeze(2).to_broadcast([P, HG, 64]), ALU.mult)
                        k3 = kt[:, 256:384].rearrange("p (g n) -> p g n", g=GKV)
                        tt(k3, k3, rs9[:, 7:9].unsqueeze(2).to_broadcast([P, GKV, 64]),
                           ALU.mult)
                        dve.drain()
                        dve.sem_inc(k_ready, 1)

                norm_x(0)
                hT_copy(0)
                for t in range(NT):
                    if t + 1 < NT:
                        norm_x(t + 1)
                    z_block(t, 0)
                    z_block(t, 1)
                    z_block(t, 2)
                    if t + 1 < NT:
                        hT_copy(t + 1)
                    z_block(t, 3)

                lp = lam_in[:].rearrange("p (a k n) -> p a k n", a=2, k=2)
                lw = rope_c[:, 0:64].rearrange("p (a n) -> p a n", a=2)
                tt(lw, lp[:, :, 0, :], lp[:, :, 1, :], ALU.mult)
                dve.drain()
                red(lam4[:, 0:2], lw, AX.X, ALU.add).then_inc(lam_s, 1)
                dve.wait_ge(lam_e, l + 1)
                tt(lam, lam4[:, 2:3], lam4[:, 3:4], ALU.subtract)
                ts(df_g[:], df_g[:], lconst[:, 1:2], None, ALU.mult)
                dve.drain()
                tt(lam, lam, lconst[:, 0:1], ALU.add)
                dve.drain()

                def query_copies(gb):
                    b = gb % 8
                    dve.wait_ge(qt_done, l * N_Q + gb + 1)
                    src = ps[:, 7, (gb % 2) * P:(gb % 2 + 1) * P]
                    if b < 6:
                        cp(pair_q[b % 2][0][0:64, :], src[0:64, :]).then_inc(qz_d, 1)
                    else:
                        cp(quad_q[b % 2][0][0:32, :], src[0:32, :])
                        cp(quad_q[b % 2][1][32:64, :], src[32:64, :]).then_inc(qz_d, 1)

                def sum_reciprocal(n):
                    t, h = divmod(n, N_UNIT)
                    column = h + N_UNIT * (t % 2)
                    dve.reciprocal(rec[:, n % 2:n % 2 + 1], sums[:, column:column + 1])

                def row_max(n):
                    t, h = divmod(n, N_UNIT)
                    dve.wait_ge(s_done, l * N_S + n + 1)
                    b0 = 2 * (n % 2)
                    if t == 0:
                        red(mx[:, n % 2:n % 2 + 1], ps[:, b0, 0:P], AX.X, ALU.max)
                    else:
                        red(mx[:, n % 2:n % 2 + 1], ps[:, b0:b0 + 2, 0:384], AX.XY, ALU.max)
                    if n >= 2:
                        dve.wait_ge(exp_done, l * N_S + n - 1)
                        sum_reciprocal(n - 2)
                    dve.drain()
                    ts(negm[:, n % 2:n % 2 + 1], mx[:, n % 2:n % 2 + 1], -score_map(h)[4], None,
                       ALU.mult).then_inc(m_ready, 1)

                def probsT(n):
                    if n < N_UNIT:
                        return
                    dve.wait_ge(pt4_done, l * N_S + n + 1)
                    dve.wait_ge(pv_done, l * N_S + n - 1)
                    cp(prT[n % 2][:, 0:384], ps[:, 4, 0:384]).then_inc(pt4_evac, 1)

                def head_out(n):
                    t, h = divmod(n, N_UNIT)
                    c = out_column(h)
                    m = h - HM - HG
                    r = rec[:, n % 2:n % 2 + 1]
                    dve.wait_ge(pv_done, l * N_S + n + 1)
                    if n + 2 >= N_S:
                        sum_reciprocal(n)
                        dve.drain()
                    O = ps[:, 6, (n % 2) * 64:(n % 2 + 1) * 64]
                    dst = q_tok[t][:, c:c + 64]
                    if m >= 0 and m % 2 == 1:
                        stt(r, r, -1.0, lam, ALU.mult, ALU.mult)
                        dve.drain()
                        stt(dst, O, r, dst, ALU.mult, ALU.add).then_inc(o_evac, 1)
                        dve.drain()
                    else:
                        ts(dst, O, r, None, ALU.mult).then_inc(o_evac, 1)
                        if m >= 0:
                            dve.drain()

                def diff_sums(t):
                    od = q_tok[t][:, 768:1024]
                    sq = k_tok[:, 256:512]
                    tt(sq, od, od, ALU.mult)
                    dve.drain()
                    red(ss4, sq.rearrange("p (h n) -> p h n", h=HD), AX.X, ALU.add)
                    dve.drain()
                    ts(ss4, ss4, 1.0 / 64, None, ALU.mult).then_inc(ss4_ready, 1)

                def diff_norm(t):
                    od = q_tok[t][:, 768:1024].rearrange("p (h n) -> p h n", h=HD)
                    dve.wait_ge(rs4_ready, l * NT + t + 1)
                    tt(od, od, rs4.unsqueeze(2).to_broadcast([P, HD, 64]), ALU.mult)
                    dve.drain()
                    tt(od, od, df_g[:].unsqueeze(1).to_broadcast([P, HD, 64]), ALU.mult).then_inc(o_ready, 1)

                for n in range(N_S + 2):
                    if n < N_S:
                        h = n % N_UNIT
                        b = score_map(h)[0]
                        if h == MAPS_OF_BLOCK[b][0]:
                            gb = 8 * (n // N_UNIT) + b
                            if gb == 0:
                                query_copies(0)
                            if gb + 1 < N_Q:
                                query_copies(gb + 1)
                        row_max(n)
                    if 1 <= n <= N_S:
                        probsT(n - 1)
                    if n >= 2:
                        head_out(n - 2)
                        if (n - 2) % N_UNIT == N_UNIT - 1 and n < N_S:
                            diff_sums((n - 2) // N_UNIT)
                    if n >= 4 and (n - 4) % N_UNIT == N_UNIT - 1:
                        diff_norm((n - 4) // N_UNIT)

                def oT_copy(t):
                    dve.wait_ge(oT_done, l * 2 * NT + 2 * t + 1)
                    cp(hT[:, 0:4, t * P:(t + 1) * P],
                       ps[:, 4, :].rearrange("p (c n) -> p c n", c=4)).then_inc(oT_evac_d, 1)

                oT_copy(0)
                diff_sums(NT - 1)
                diff_norm(NT - 1)

                def x_add(t, b):
                    c0, c1 = WO_COLS[b]
                    n = 3 * t + b
                    if n == 0:
                        dve.wait_ge(s_gate1, (l + 1) * 32)
                        dve.wait_ge(s_fill, 16)
                    dve.wait_ge(wo_done, l * 15 + n + 1)
                    tt(xo_tmp[:, 0:c1 - c0], ps[:, n % 4, 0:c1 - c0], (gate1l if t else gate1c)[:, c0:c1], ALU.mult)
                    dve.drain()
                    tt(x_t[t][:, c0:c1], x_t[t][:, c0:c1], xo_tmp[:, 0:c1 - c0], ALU.add).then_inc(xo_done, 1)
                    dve.drain()

                def mixer_in(t):
                    k = min(t, 1)
                    if t == 0:
                        dve.wait_ge(s_bcast, (l + 1) * (16 * 7))
                        for q in range(2):
                            stt(a2b[:, q, :], a2b[:, q, :], 1.0, gain_b, ALU.add, ALU.mult)
                        dve.drain()
                    dve.wait_ge(rs2_ready, l * NT + t + 1)
                    stt(h2, x_t[t], rs2[:, t:t + 1], a2b[:, k, :], ALU.mult, ALU.mult)
                    dve.drain()
                    tt(h2, h2, b2b[:, k, :], ALU.add).then_inc(h2_ready, 1)

                def h2T_copy(t):
                    dve.wait_ge(h2T_done, l * 2 * NT + 2 * t + 1)
                    if t >= 1:
                        dve.wait_ge(rt_done, l * NT + t)
                    cp(h2T[:, 0:4, :], ps[:, 6, :].rearrange("p (c n) -> p c n", c=4)).then_inc(h2T_evac_d, 1)

                def logits_in(t):
                    dve.wait_ge(rt_done, l * NT + t + 1)
                    tt(logits[:, t, :], ps[:, 6, 0:20], b_rt[:], ALU.add).then_inc(lg_ready, 1)

                for t in range(NT):
                    x_add(t, 0)
                    if t >= 1:
                        h2T_copy(t - 1)
                    if t + 1 < NT:
                        oT_copy(t + 1)
                    x_add(t, 1)
                    if t >= 1:
                        logits_in(t - 1)
                    x_add(t, 2)
                    mixer_in(t)
                h2T_copy(NT - 1)
                logits_in(NT - 1)
                dve.drain()

                dve.wait_ge(s_hout, l * 80 + 80)
                G, E = logits[:, :, 0:4], logits[:, :, 4:20]

                def bc(v, n):
                    return v.unsqueeze(2).to_broadcast([P, NT, n])

                def first_of(vals, top, out):
                    tt(v3(r_t1, 4), vals, bc(top, 4), ALU.is_equal)
                    dve.drain()
                    tt(v3(r_t2, 4), v3(r_t1, 4), desc[:].unsqueeze(1).to_broadcast([P, NT, 4]), ALU.mult)
                    dve.drain()
                    red(r_t3, v3(r_t2, 4), AX.X, ALU.max)
                    dve.drain()
                    tt(v3(out, 4), v3(r_t2, 4), bc(r_t3, 4), ALU.is_equal)
                    dve.drain()

                red(r_gm, G, AX.X, ALU.max)
                dve.drain()
                tt(v3(r_gs, 4), G, bc(r_gm, 4), ALU.subtract).then_inc(r_sub, 1)
                first_of(G, r_gm, r_og)
                tt(v4(r_sel), E.rearrange("p t (g e) -> p t g e", g=NGRP),
                   v3(r_og, 4).unsqueeze(3).to_broadcast([P, NT, NGRP, EPG]), ALU.mult)
                dve.drain()
                red(v3(r_es, 4), r_sel.rearrange("p (t g e) -> p t e g", t=NT, g=NGRP), AX.X, ALU.add)
                dve.drain()
                red(r_m1, v3(r_es, 4), AX.X, ALU.max)
                dve.drain()
                first_of(v3(r_es, 4), r_m1, r_o1)
                stt(r_es2, r_o1, -3.0e38, r_es, ALU.mult, ALU.add)
                dve.drain()
                red(r_m2, v3(r_es2, 4), AX.X, ALU.max)
                dve.drain()
                tt(r_d, r_m2, r_m1, ALU.subtract).then_inc(r_sub, 1)
                first_of(v3(r_es2, 4), r_m2, r_o2)
                for O_, o_ in ((r_O1, r_o1), (r_O2, r_o2)):
                    tt(v4(O_), v3(r_og, 4).unsqueeze(3).to_broadcast([P, NT, NGRP, EPG]),
                       v3(o_, 4).unsqueeze(2).to_broadcast([P, NT, NGRP, EPG]), ALU.mult)
                dve.drain()
                tt(r_M, r_O1, r_O2, ALU.add).then_inc(r_mask, 1)
                dve.wait_ge(r_exp, 2 * l + 2)
                red(r_gtop, v3(r_gex, 4), AX.X, ALU.add)
                ts(r_den, r_ex2, 1.0, None, ALU.add)
                dve.drain()
                tt(r_den, r_den, r_gtop, ALU.mult)
                dve.drain()
                dve.reciprocal(rout_w[:, 0:NT], r_den)
                dve.drain()
                tt(rout_w[:, NT:2 * NT], rout_w[:, 0:NT], r_ex2, ALU.mult)
                dve.wait_ge(r_count, l + 1)
                cp(r_cn, ps[:, 6, 128:208])
                cp(r_rank, ps[:, 6, 256:336])
                dve.drain()
                big4 = r_big.rearrange("p (t e s) -> p t e s", t=NT, e=NE)
                tt(big4, r_cn.rearrange("p (s e) -> p e s", e=NE).unsqueeze(1).to_broadcast([P, NT, NE, NT]),
                   v3(lt[:], NT).unsqueeze(2).to_broadcast([P, NT, NE, NT]), ALU.mult)
                red(r_c, r_cn.rearrange("p (s e) -> p e s", e=NE), AX.X, ALU.add)
                dve.drain()
                red(v3(r_add, NE), big4, AX.X, ALU.add)
                dve.drain()
                tt(r_rank, r_rank, r_add, ALU.add)
                b3 = r_big[:, 0:NE * NT].rearrange("p (e s) -> p e s", e=NE)
                tt(b3, r_c.unsqueeze(2).to_broadcast([P, NE, NT]),
                   k128[:].unsqueeze(1).to_broadcast([P, NE, NT]), ALU.is_gt)
                dve.drain()
                red(r_nt, b3, AX.X, ALU.add)
                dve.drain()
                b5 = r_big[:, 0:NE * NE].rearrange("p (e s) -> p e s", e=NE)
                tt(b5, r_nt.unsqueeze(1).to_broadcast([P, NE, NE]),
                   le[:].rearrange("p (e s) -> p e s", e=NE), ALU.mult)
                dve.drain()
                red(r_incl, b5, AX.X, ALU.add)
                dve.drain()
                b6 = r_big[0:1, 0:N_ET * NE].rearrange("p (i e) -> p i e", e=NE)
                tt(b6, r_incl[0:1, :].unsqueeze(1).to_broadcast([1, N_ET, NE]),
                   iota_t[0:1, :].unsqueeze(2).to_broadcast([1, N_ET, NE]), ALU.is_le)
                tt(r_excl, r_incl, r_nt, ALU.subtract)
                dve.drain()
                red(r_ex[0:1, :], b6, AX.X, ALU.add)
                stt(v3(r_rank, NE), r_excl.unsqueeze(1).to_broadcast([P, NT, NE]), float(P), v3(r_rank, NE),
                    ALU.mult, ALU.add)
                dve.drain()
                cp(experts_i[0:1, N_ET:N_ET + 1], r_incl[0:1, NE - 1:NE])
                dve.drain()
                ts(experts_i[0:1, 0:N_ET], r_ex[0:1, :], float(NE - 1), None, ALU.min).then_inc(experts_ready, 1)
                tt(r_O1, r_O1, r_rank, ALU.mult)
                tt(r_O2, r_O2, r_rank, ALU.mult)
                dve.drain()
                red(r_sl[:, 0:NT], v3(r_O1, NE), AX.X, ALU.add)
                red(r_sl[:, NT:2 * NT], v3(r_O2, NE), AX.X, ALU.add)
                dve.drain()
                def by_tile(v):
                    return v.unsqueeze(2).to_broadcast([P, 2 * NT, N_ET])
                tiles = iota_t[:].unsqueeze(1).to_broadcast([P, 2 * NT, N_ET])
                cp(slots_i[:], r_sl).then_inc(slots_ready, 1)
                ts(r_tl, r_sl, 1.0 / P, None, ALU.mult)
                dve.drain()
                tt(tile_hot, by_tile(r_tl), tiles, ALU.is_ge)
                dve.drain()
                red(r_tl, tile_hot, AX.X, ALU.add)
                dve.drain()
                ts(r_tl, r_tl, -1.0, None, ALU.add)
                dve.drain()
                stt(r_sl, r_tl, -float(P), r_sl, ALU.mult, ALU.add)
                tt(tile_hot, by_tile(r_tl), tiles, ALU.is_equal)
                dve.drain()
                tt(place_hot, r_sl.unsqueeze(2).to_broadcast([P, 2 * NT, P]),
                   lane[:].unsqueeze(1).to_broadcast([P, 2 * NT, P]), ALU.is_equal)
                tok = tok_id[:].unsqueeze(2).to_broadcast([P, NT, N_ET])
                for k in range(2):
                    last = tt(pair_tok[:, k * NT:(k + 1) * NT, :], tile_hot[:, k * NT:(k + 1) * NT, :], tok, ALU.mult)
                last.then_inc(r_hot, 1)
                dve.wait_ge(r_rows, l + 1)
                cp(idx[:], ps[:, 6, 352:352 + N_ET]).then_inc(idx_ready, 1)

                def rows_in(i):
                    with if_used(dve, i):
                        dve.wait_ge(gt_done[l], i + 1)
                        if i >= 2:
                            dve.wait_ge(gu_done[l], i - 1)
                        cp(hgT[i % 2][:, 0:4, :], ps[:, 0, :].rearrange("p (c n) -> p c n", c=4)).then_inc(gt_evac_d[l], 1)

                def hidden(i):
                    with if_used(dve, i):
                        G_ = ps[:, 2 + i % 2, :]
                        dve.wait_ge(sig_done[l], i + 1)
                        ts(sig[i % 2], sig[i % 2], 1.0, None, ALU.add)
                        dve.drain()
                        dve.reciprocal(sig[i % 2], sig[i % 2])
                        dve.drain()
                        tt(sig[i % 2], sig[i % 2], G_[:, 0:FF], ALU.mult)
                        dve.drain()
                        if i >= 2:
                            dve.wait_ge(ht_done[l], i - 1)
                        tt(hid[i % 2], sig[i % 2], G_[:, FF:2 * FF], ALU.mult).then_inc(hid_ready[l], 1)

                def hiddenT(i):
                    with if_used(dve, i):
                        dve.wait_ge(ht_done[l], i + 1)
                        if i >= 2:
                            dve.wait_ge(dn_done[l], i - 1)
                        cp(hidT[i % 2], ps[:, 4, 0:FF].rearrange("p (c n) -> p c n", c=2)).then_inc(ht_evac[l], 1)

                def y_copy(i):
                    with if_used(dve, i):
                        dve.wait_ge(dn_done[l], i + 1)
                        y_buffer_free(dve, l, i)
                        cp(y_out[i % 2][:, 0:512], ps[:, 5, :]).then_inc(y_evac_d[l], 1)

                load_tiles_used(dve, l)
                rows_in(0)
                for i in range(N_ET + 1):
                    if i >= 1:
                        hiddenT(i - 1)
                    if i < N_ET:
                        hidden(i)
                    if i + 1 < N_ET:
                        rows_in(i + 1)
                    if i >= 1:
                        y_copy(i - 1)

                for t in range(NT):
                    dve.wait_ge(s_yin[t], l * 32 + 32)
                    dve.wait_ge(y1_ready, l * NT + t + 1)
                    y1, y2 = y_in[t]
                    stt(y1, y2, rout_w[:, NT + t:NT + t + 1], y1, ALU.mult, ALU.add)
                    dve.drain()
                    tt(y1, y1, gate2b[:, min(t, 1), :], ALU.mult)
                    dve.drain()
                    tt(x_t[t], x_t[t], y1, ALU.add).then_inc(x_ready, 1)
                    dve.drain()
                    if l == DEPTH - 1 and t >= 2:
                        final_scale(t - 2)

            for t in (NT - 2, NT - 1):
                final_scale(t)

        @block.tensor
        def _(pe):
            mm = pe.matmul

            def tr(out, in_):
                return pe.transpose(out, in_, ident[:])
            pe.sem_inc(k2_done, 1)
            pe.sem_inc(hT_evac, 1)
            pe.sem_inc(kA_evac, 1)
            pe.sem_inc(kB_evac, 1)
            pe.wait_ge(c_cond, 1)

            def mod_chunk(l, j):
                g = USE_AT["mod", l, j]
                pe.wait_ge(w_landed[g % RING], USE_CUM[g])
                if l * N_MOD + j >= 1:
                    pe.wait_ge(mod_evac, max(l * N_MOD + j - 1, 1))
                w = slot[g % RING].rearrange("p (c n) -> p c n", c=KC)
                for c in range(KC):
                    last = mm(ps[0:2, 2 + j % 2, :], silu_v[:, :, c], w[:, c, :],
                              start=(c == 0), stop=(c == KC - 1))
                last.then_inc(mod_done, 1)

            for j in range(N_MOD):
                mod_chunk(0, j)
            pe.wait_ge(c_const, 1)

            for l in range(DEPTH):
                w_slots = {}

                def landed(kind, i):
                    g = USE_AT[kind, l, i]
                    pe.wait_ge(w_landed[g % RING], USE_CUM[g])
                    return slot[g % RING]

                def hT_round(t, r):
                    pe.wait_ge(xn_ready, l * NT + t + 1)
                    pe.wait_ge(hT_evac, l * 2 * NT + 2 * t + r + 1)
                    for q in range(4):
                        last = tr(ps[:, 7, q * P:(q + 1) * P], xn[t % 2][:, 4 * r + q:D:KC])
                    last.then_inc(hT_done, 1)

                def z_block(t, b):
                    if t == 0:
                        w_slots["in", b] = landed("in", b)
                        if b == 0:
                            pe.wait_ge(mod_evac, (l + 1) * N_MOD)
                        pe.wait_ge(hT_evac, l * 2 * NT + 3)
                    else:
                        pe.wait_ge(z_used_d, l * 4 * NT + 4 * (t - 1) + b + 1)
                        if b != 1:
                            pe.wait_ge(z_used_a, l * 3 * NT + 3 * (t - 1) + (1, 0, 2, 3)[b])
                        pe.wait_ge(hT_evac, l * 2 * NT + 2 * t + 3)
                    n = BLK[b][1] - BLK[b][0]
                    w = w_slots["in", b][:, 0:KC * n].rearrange("p (c n) -> p c n", c=KC)
                    for c in range(KC):
                        last = mm(ps[:, b, 0:n], hT[:, c, t * P:(t + 1) * P], w[:, c, :],
                                  start=(c == 0), stop=(c == KC - 1))
                    last.then_inc(z_done, 1)

                def keys1(u):
                    kt = k_view[u % 2]
                    if u < 2:
                        pe.wait_ge(s_small, (l + 1) * (16 * N_SMALL_IN))
                    else:
                        pe.wait_ge(k_ready, l * NT + u - 1)
                    pe.wait_ge(kA_evac, l * NU + u + 1)
                    tr(ps[:, 4, 0:128], kt[:, 0:128])
                    tr(ps[:, 4, 128:256], kt[:, 256:384])
                    tr(ps[:, 4, 256:384], kt[:, 384:512])
                    tr(ps[:, 4, 384:512], kt[:, 512:640]).then_inc(k1_done, 1)

                def keys2(u):
                    kt = k_view[u % 2]
                    pe.wait_ge(kA_evac, l * NU + u + 2)
                    pe.wait_ge(kB_evac, l * NU + u + 1)
                    for j in range(3):
                        mm(ps[:, 5, j * P:(j + 1) * P], wuk[:, j * P:(j + 1) * P], ckvT[:], start=True, stop=False)
                        mm(ps[:, 5, j * P:(j + 1) * P], kt[:, 128:256], ident[:], start=False, stop=True)
                    mm(ps[:, 6, 0:384], ckvT[:], wuv[:], start=True, stop=True).then_inc(k2_done, 1)

                hT_round(0, 0)
                hT_round(0, 1)
                for u in range(2):
                    keys1(u)
                    keys2(u)
                for t in range(NT):
                    z_block(t, 0)
                    if t >= 1:
                        keys1(1 + t)
                    z_block(t, 1)
                    z_block(t, 2)
                    if t >= 1:
                        keys2(1 + t)
                    if t + 1 < NT:
                        hT_round(t + 1, 0)
                    z_block(t, 3)
                    if t + 1 < NT:
                        hT_round(t + 1, 1)
                keys1(NU - 1)
                keys2(NU - 1)

                def query_block(gb):
                    t, b = divmod(gb, 8)
                    if gb == 0:
                        pe.wait_ge(k_ready, l * NT + NT)
                        pe.wait_ge(z_used_a, (l + 1) * (3 * NT))
                        pe.wait_ge(hT_evac, (l + 1) * (2 * NT) + 1)
                    if gb >= 1:
                        pe.wait_ge(qz_d, l * N_Q + gb)
                        pe.wait_ge(qz_a, l * N_Q + gb)
                    tr(ps[:, 7, (gb % 2) * P:(gb % 2 + 1) * P],
                       q_tok[t][:, b * P:(b + 1) * P]).then_inc(qt_done, 1)

                def scores(n):
                    t, h = divmod(n, N_UNIT)
                    b, part, plane, _, _ = score_map(h)
                    if n == 0:
                        pe.wait_ge(kB_evac, (l + 1) * NU + 1)
                        pe.wait_ge(z_used_d, (l + 1) * (4 * NT))
                    pe.wait_ge(qz_d, l * N_Q + 8 * t + b + 1)
                    pe.wait_ge(qz_a, l * N_Q + 8 * t + b + 1)
                    if n >= 2:
                        pe.wait_ge(exp_done, l * N_S + n - 1)
                    q = (pair_q if b < 6 else quad_q)[b % 2][part]
                    b0 = 2 * (n % 2)
                    if t == 0:
                        mm(ps[:, b0, 0:P], q, kT[:, plane, 768:896], start=True, stop=True).then_inc(s_done, 1)
                    else:
                        mm(ps[:, b0, 0:384], q, kT[:, plane, 0:384], start=True, stop=True)
                        mm(ps[:, b0 + 1, 0:384], q, kT[:, plane, 384:768], start=True, stop=True).then_inc(s_done, 1)

                def probsT(n):
                    pe.wait_ge(exp_done, l * N_S + n + 1)
                    if n >= 1:
                        pe.wait_ge(pt4_evac, l * N_S + n)
                    else:
                        pe.wait_ge(kA_evac, (l + 1) * NU + 1)
                    if n < N_UNIT:
                        tr(ps[:, 4, 0:P], pr[n % 2][:, 0:P]).then_inc(pt4_done, 1)
                        return
                    for c in range(3):
                        last = tr(ps[:, 4, c * P:(c + 1) * P], pr[n % 2][:, c * P:(c + 1) * P])
                    last.then_inc(pt4_done, 1)
                    if n > N_UNIT:
                        pe.wait_ge(pt5_evac, l * N_S5 + n - N_UNIT)
                    for c in range(3):
                        last = tr(ps[:, 5, c * P:(c + 1) * P], pr[n % 2][:, (3 + c) * P:(4 + c) * P])
                    last.then_inc(pt5_done, 1)

                def values(n):
                    t, h = divmod(n, N_UNIT)
                    vc = score_map(h)[3]
                    pe.wait_ge(pt4_evac, l * N_S + n + 1)
                    if t >= 1:
                        pe.wait_ge(pt5_evac, l * N_S5 + n - N_UNIT + 1)
                        if n == N_UNIT:
                            pe.wait_ge(s_vcache, l * 32 + 32)
                    pe.wait_ge(o_evac, l * N_S + n + 1)
                    units = [2] if t == 0 else SEEN
                    for c, u in enumerate(units):
                        last = mm(ps[:, 6, (n % 2) * 64:(n % 2 + 1) * 64], prT[n % 2][:, c * P:(c + 1) * P],
                                  V[:, u, vc:vc + 64], start=(c == 0), stop=(c == len(units) - 1))
                    last.then_inc(pv_done, 1)

                for n in range(N_S + 2):
                    if n < N_S:
                        h = n % N_UNIT
                        b = score_map(h)[0]
                        if h == MAPS_OF_BLOCK[b][0]:
                            gb = 8 * (n // N_UNIT) + b
                            if gb == 0:
                                query_block(0)
                            if gb + 1 < N_Q:
                                query_block(gb + 1)
                        scores(n)
                    if 1 <= n <= N_S:
                        probsT(n - 1)
                    if n >= 2:
                        values(n - 2)

                def oT_round(t, r):
                    pe.wait_ge(o_ready, l * NT + t + 1)
                    if t >= 1:
                        pe.wait_ge((oT_evac_d, oT_evac_a)[r], l * NT + t)
                    else:
                        pe.wait_ge(pt4_evac, l * N_S + N_S)
                        pe.wait_ge(pt5_evac, l * N_S5 + N_S5)
                    for q in range(4):
                        last = tr(ps[:, 4 + r, q * P:(q + 1) * P], q_tok[t][:, 4 * r + q:D:KC])
                    last.then_inc(oT_done, 1)

                def out_block(t, b):
                    n = 3 * t + b
                    if t == 0:
                        w_slots["out", b] = landed("out", b)
                    if n >= 4:
                        pe.wait_ge(xo_done, l * 15 + n - 3)
                    else:
                        pe.wait_ge(exp_done, (l + 1) * N_S)
                    pe.wait_ge(oT_evac_d, l * NT + t + 1)
                    pe.wait_ge(oT_evac_a, l * NT + t + 1)
                    w_ = WO_COLS[b][1] - WO_COLS[b][0]
                    w = w_slots["out", b][:, 0:KC * w_].rearrange("p (c n) -> p c n", c=KC)
                    for c in range(KC):
                        last = mm(ps[:, n % 4, 0:w_], hT[:, c, t * P:(t + 1) * P], w[:, c, :],
                                  start=(c == 0), stop=(c == KC - 1))
                    last.then_inc(wo_done, 1)

                def h2T_rounds(t):
                    pe.wait_ge(h2_ready, l * NT + t + 1)
                    if t == 0:
                        pe.wait_ge(o_evac, (l + 1) * N_S + 1)
                        pe.wait_ge(qz_d, (l + 1) * N_Q)
                        pe.wait_ge(qz_a, (l + 1) * N_Q)
                    else:
                        pe.wait_ge(lg_ready, l * NT + t)
                        pe.wait_ge(h2T_evac_a, l * NT + t)
                    for r in range(2):
                        for q in range(4):
                            last = tr(ps[:, 6 + r, q * P:(q + 1) * P], h2[:, 4 * r + q:D:KC])
                        last.then_inc(h2T_done, 1)

                def router(t):
                    pe.wait_ge(h2T_evac_d, l * NT + t + 1)
                    pe.wait_ge(h2T_evac_a, l * NT + t + 1)
                    w = w_rt[:].rearrange("p (c n) -> p c n", c=KC)
                    for c in range(KC):
                        last = mm(ps[:, 6, 0:20], h2T[:, c, :], w[:, c, :], start=(c == 0), stop=(c == KC - 1))
                    last.then_inc(rt_done, 1)

                oT_round(0, 0)
                oT_round(0, 1)
                for t in range(NT):
                    out_block(t, 0)
                    if t + 1 < NT:
                        oT_round(t + 1, 0)
                    if t >= 1:
                        h2T_rounds(t - 1)
                    out_block(t, 1)
                    if t + 1 < NT:
                        oT_round(t + 1, 1)
                    if t >= 1:
                        router(t - 1)
                    out_block(t, 2)
                h2T_rounds(NT - 1)
                router(NT - 1)
                pe.wait_ge(xo_done, l * 15 + 15)
                if l + 1 < DEPTH:
                    mod_chunk(l + 1, 0)
                pe.wait_ge(r_mask, l + 1)
                pe.wait_ge(lg_ready, l * NT + NT)
                mm(ps[:, 6, 128:208], ones[:], r_M, start=True, stop=True)
                mm(ps[:, 6, 256:336], tri[:], r_M, start=True, stop=True).then_inc(r_count, 1)
                if l + 1 < DEPTH:
                    mod_chunk(l + 1, 1)
                    mod_chunk(l + 1, 2)
                pe.wait_ge(r_hot, l + 1)
                for k in range(2 * NT):
                    last = mm(ps[:, 6, 352:352 + N_ET], place_hot[:, k, :], pair_tok[:, k, :],
                              start=(k == 0), stop=(k == 2 * NT - 1))
                last.then_inc(r_rows, 1)

                def rows_T(i):
                    with if_used(pe, i):
                        pe.wait_ge(s_hg[l][i % 2], 16 * (i // 2 + 1))
                        if i >= 1:
                            pe.wait_ge(gt_evac_d[l], i)
                            pe.wait_ge(gt_evac_a[l], i)
                        else:
                            pe.wait_ge(xo_done, l * 15 + 15)
                        for c in range(KC):
                            last = tr(ps[:, c // 4, (c % 4) * P:(c % 4 + 1) * P], hg[i % 2][:, c:D:KC])
                        last.then_inc(gt_done[l], 1)

                def gate_up(i):
                    with if_used(pe, i):
                        pe.wait_ge(wgu_landed[l][i % RING], 32 * (i // RING + 1))
                        w = slot[USE_AT["moe", l, i] % RING].rearrange("p (c n) -> p c n", c=KC)
                        pe.wait_ge(gt_evac_d[l], i + 1)
                        pe.wait_ge(gt_evac_a[l], i + 1)
                        if i >= 2:
                            pe.wait_ge(hid_ready[l], i - 1)
                        elif l + 1 < DEPTH:
                            pe.wait_ge(mod_evac, (l + 1) * N_MOD + MOD_MID)
                        for c in range(KC):
                            last = mm(ps[:, 2 + i % 2, :], hgT[i % 2][:, c, :], w[:, c, :],
                                      start=(c == 0), stop=(c == KC - 1))
                        last.then_inc(gu_done[l], 1)

                def hidden_T(i):
                    with if_used(pe, i):
                        pe.wait_ge(hid_ready[l], i + 1)
                        if i >= 1:
                            pe.wait_ge(ht_evac[l], i)
                        for c in range(2):
                            last = tr(ps[:, 4, c * P:(c + 1) * P], hid[i % 2][:, c:FF:2])
                        last.then_inc(ht_done[l], 1)

                def down(i):
                    with if_used(pe, i):
                        pe.wait_ge(wd_landed[l][i % 2], 16 * (i // 2 + 1))
                        pe.wait_ge(ht_evac[l], i + 1)
                        if i >= 1:
                            pe.wait_ge(y_evac_d[l], i)
                            pe.wait_ge(y_evac_a[l], i)
                        w = w_dn[i % 2].rearrange("p (c n) -> p c n", c=2)
                        for k in range(2):
                            for c in range(2):
                                last = mm(ps[:, 5 + k, :], hidT[i % 2][:, c, :], w[:, c, k * 512:(k + 1) * 512],
                                          start=(c == 0), stop=(c == 1))
                        last.then_inc(dn_done[l], 1)

                if l + 1 < DEPTH:
                    for j in range(3, MOD_MID):
                        mod_chunk(l + 1, j)
                load_tiles_used(pe, l)
                rows_T(0)
                for i in range(N_ET + 1):
                    if i >= 1:
                        hidden_T(i - 1)
                    if i < N_ET:
                        gate_up(i)
                    if i + 1 < N_ET:
                        rows_T(i + 1)
                    if i >= 1:
                        down(i - 1)
                if l + 1 < DEPTH:
                    for j in range(MOD_MID, N_MOD):
                        mod_chunk(l + 1, j)


_INS = ['x_prompt', 'x_sample', 'c', 'cache_mla_ckv', 'cache_mla_krope', 'cache_gqa_k', 'cache_gqa_v',
        'cache_diff_k', 'cache_diff_v', 'c_ctx', 'norm1_g', 'norm2_g', 'w_mod', 'b_mod', 'w_in',
        'mla_kv_norm_g', 'mla_w_uk', 'mla_w_uv', 'gqa_q_norm_g', 'gqa_k_norm_g', 'diff_lambda', 'diff_norm_g',
        'w_out', 'moe_w_group', 'moe_b_group', 'moe_w_router', 'moe_b_router', 'moe_w_gate', 'moe_w_up',
        'moe_w_down', 'final_norm_g']

_OUTS = [('y_prompt', (1, T_CTX, D)), ('y_sample', (1, T_LAT, D)),
         ('new_mla_ckv', (1, DEPTH, T_CTX, RANK)), ('new_mla_krope', (1, DEPTH, T_CTX, 32)),
         ('new_gqa_k', (1, DEPTH, T_CTX, GKV, 64)), ('new_gqa_v', (1, DEPTH, T_CTX, GKV, 64)),
         ('new_diff_k', (1, DEPTH, T_CTX, HD, 2, 32)), ('new_diff_v', (1, DEPTH, T_CTX, HD, 64))]


def _rope_table():
    tab = np.zeros((NT * P, 96), np.float32)
    tab[:, 0:16] = 1.0
    tab[:, 32:64] = 1.0
    n = np.arange(T_LAT)
    row, col = (n // GRID_W).astype(np.float32), (n % GRID_W).astype(np.float32)
    for rot, c0 in ((32, 0), (64, 32)):
        quarter = rot // 4
        inv = (np.float32(ROPE_THETA) ** (-np.arange(quarter, dtype=np.float32) / np.float32(quarter))).astype(np.float32)
        ang = np.concatenate([row[:, None] * inv, col[:, None] * inv], axis=-1)
        tab[T_CTX:, c0:c0 + rot // 2] = np.cos(ang)
        tab[T_CTX:, c0 + rot // 2:c0 + rot] = np.sin(ang)
    return tab


def _layer_consts():
    out = np.zeros((DEPTH, 8), np.float32)
    for i in range(DEPTH):
        lam_init = 0.8 - 0.6 * float(np.exp(-0.3 * i))
        out[i, 0], out[i, 1] = lam_init, 1.0 - lam_init
    return out


def kernel(**inputs):
    import concourse.bacc as _bacc
    from concourse.bass_utils import run_bass_kernel_spmd as _run

    nc = _bacc.Bacc("TRN2", target_bir_lowering=False, num_devices=1)
    arrays, a, o = {}, {}, {}
    given = {name: np.ascontiguousarray(inputs[name]) for name in _INS}
    given["rope_table"] = _rope_table()
    given["layer_consts"] = _layer_consts()
    for name, v in given.items():
        arrays[f"in_{name}"] = v
        a[name] = nc.dram_tensor(f"in_{name}", v.shape, mybir.dt.from_np(v.dtype), kind="ExternalInput").ap()
    for name, shape in _OUTS:
        o[name] = nc.dram_tensor(f"out_{name}", shape, F32, kind="ExternalOutput").ap()
    trunk(nc, a, o)
    r = _run(nc, [arrays], core_ids=[0])
    return tuple(r.results[0][f"out_{name}"] for name, _ in _OUTS)
```
